# Optimizing a Trainium2 kernel written in Bass

```python
import jax, jax.numpy as jnp
from jax import lax
import numpy as np

D_MODEL = 1024
BATCH = 1
SEQ = 256
DEPTH = 2

N_HEADS = 8
HEAD_DIM = 64
N_KV = 2
GROUP = N_HEADS // N_KV
ATTN_WIDTH = N_HEADS * HEAD_DIM
KV_WIDTH = N_KV * HEAD_DIM
N_BRANCH = 3
CMP_BLOCK = 32
CMP_STRIDE = 16
CMP_HIDDEN = 256
SEL_BLOCK = 64
N_SEL = 16
WINDOW = 512
Q_BLOCK = 64
FORCE_BONUS = 1e3
CONV_CH = D_MODEL - ATTN_WIDTH
CONV_WIDTH = 31
D_FF = 2816
EPS = 1e-6
SPLITS = [ATTN_WIDTH] + [KV_WIDTH] * 6 + [N_HEADS * N_BRANCH, CONV_CH, CONV_CH]
IN_WIDTH = sum(SPLITS)

kernel_name = "hymba_nsa_conformer_macaron"

def rms_norm(x, g):
    x32 = x.astype(jnp.float32)
    y = x32 * lax.rsqrt(jnp.mean(x32 * x32, axis=-1, keepdims=True) + EPS)
    return (y * g.astype(jnp.float32)).astype(x.dtype)

def layer_norm(x, g, b):
    x32 = x.astype(jnp.float32)
    mu = jnp.mean(x32, axis=-1, keepdims=True)
    var = jnp.mean(jnp.square(x32 - mu), axis=-1, keepdims=True)
    y = (x32 - mu) * lax.rsqrt(var + EPS)
    return (y * g.astype(jnp.float32) + b.astype(jnp.float32)).astype(x.dtype)

def swiglu(h, w_gate, w_up, w_down):
    return (jax.nn.silu(h @ w_gate) * (h @ w_up)) @ w_down

def alibi_slopes():
    return jnp.exp2(-8.0 * jnp.arange(1, N_HEADS + 1, dtype=jnp.float32) / N_HEADS)

def masked_softmax(s, mask):
    p = jax.nn.softmax(jnp.where(mask, s, -1e30), axis=-1)
    return p * mask.astype(p.dtype)

def compress(k, pos, w1, w2):
    B, S = k.shape[0], k.shape[1]
    chunks = k.reshape(B, S // CMP_STRIDE, CMP_STRIDE, N_KV, HEAD_DIM)
    blocks = jnp.concatenate([chunks[:, :-1], chunks[:, 1:]], axis=2)
    blocks = blocks + pos[None, None, :, None, :]
    nc = blocks.shape[1]
    flat = blocks.transpose(0, 1, 3, 2, 4).reshape(B, nc, N_KV, CMP_BLOCK * HEAD_DIM)
    return jax.nn.silu(flat @ w1) @ w2

def nsa_attention(q, k_cmp, v_cmp, k_slc, v_slc, k_win, v_win, gates,
                  pos_k, wk1, wk2, pos_v, wv1, wv2):
    B, S = q.shape[0], q.shape[1]
    scale = HEAD_DIM ** -0.5
    kc = compress(k_cmp, pos_k, wk1, wk2)
    vc = compress(v_cmp, pos_v, wv1, wv2)
    nc = kc.shape[1]
    ns = S // SEL_BLOCK
    n_sel = min(N_SEL, ns)
    cmp_start = jnp.arange(nc) * CMP_STRIDE
    cmp_end = cmp_start + CMP_BLOCK - 1
    sel_start = jnp.arange(ns) * SEL_BLOCK
    overlap = jnp.clip(jnp.minimum(cmp_start[:, None] + CMP_BLOCK, sel_start[None] + SEL_BLOCK)
                       - jnp.maximum(cmp_start[:, None], sel_start[None]), 0).astype(jnp.float32) / CMP_BLOCK
    ks_blocks = k_slc.reshape(B, ns, SEL_BLOCK, N_KV, HEAD_DIM).transpose(0, 3, 1, 2, 4)
    vs_blocks = v_slc.reshape(B, ns, SEL_BLOCK, N_KV, HEAD_DIM).transpose(0, 3, 1, 2, 4)
    pad = jnp.zeros((B, WINDOW, N_KV, HEAD_DIM), k_win.dtype)
    kw_pad = jnp.concatenate([pad, k_win], axis=1)
    vw_pad = jnp.concatenate([pad, v_win], axis=1)
    qg = q.reshape(B, S, N_KV, GROUP, HEAD_DIM)
    gg = jax.nn.sigmoid(gates.reshape(B, S, N_KV, GROUP, N_BRANCH))
    slopes = alibi_slopes().reshape(N_KV, GROUP)[None, :, :, None, None]
    bidx = jnp.arange(B)[:, None, None, None]
    gidx = jnp.arange(N_KV)[None, :, None, None]
    sel_offs = jnp.arange(SEL_BLOCK)
    win_offs = jnp.arange(Q_BLOCK + WINDOW) - WINDOW
    blk = jnp.arange(ns)

    def chunk(c):
        q0 = c * Q_BLOCK
        qc = lax.dynamic_slice_in_dim(qg, q0, Q_BLOCK, axis=1)
        gc = lax.dynamic_slice_in_dim(gg, q0, Q_BLOCK, axis=1)
        t = q0 + jnp.arange(Q_BLOCK)
        m_c = cmp_end[None, :] <= t[:, None]
        d_c = (t[:, None] - cmp_end[None, :]).astype(jnp.float32)
        s_c = jnp.einsum('bqgrd,bngd->bgrqn', qc, kc, preferred_element_type=jnp.float32) * scale - slopes * d_c
        p_c = masked_softmax(s_c, m_c)
        o_cmp = jnp.einsum('bgrqn,bngd->bqgrd', p_c.astype(vc.dtype), vc)
        imp = jnp.einsum('bgrqn,nj->bgqj', p_c, overlap)
        tb = t // SEL_BLOCK
        forced = (blk[None] == 0) | (blk[None] == tb[:, None]) | (blk[None] == tb[:, None] - 1)
        valid = blk[None] * SEL_BLOCK <= t[:, None]
        score = jnp.where(valid, imp + jnp.where(forced, FORCE_BONUS, 0.0), -jnp.inf)
        _, idx = lax.top_k(score, n_sel)
        kg = ks_blocks[bidx, gidx, idx].reshape(B, N_KV, Q_BLOCK, n_sel * SEL_BLOCK, HEAD_DIM)
        vg = vs_blocks[bidx, gidx, idx].reshape(B, N_KV, Q_BLOCK, n_sel * SEL_BLOCK, HEAD_DIM)
        pos = (idx[..., None] * SEL_BLOCK + sel_offs).reshape(B, N_KV, Q_BLOCK, n_sel * SEL_BLOCK)
        d_s = (t[None, None, :, None] - pos)[:, :, None]
        s_s = jnp.einsum('bqgrd,bgqkd->bgrqk', qc, kg, preferred_element_type=jnp.float32) \
            - slopes * d_s.astype(jnp.float32)
        s_s = s_s * 1.0 if False else s_s
        s_s = jnp.einsum('bqgrd,bgqkd->bgrqk', qc, kg, preferred_element_type=jnp.float32) * scale \
            - slopes * d_s.astype(jnp.float32)
        p_s = masked_softmax(s_s, d_s >= 0)
        o_slc = jnp.einsum('bgrqk,bgqkd->bqgrd', p_s.astype(vg.dtype), vg)
        kw = lax.dynamic_slice_in_dim(kw_pad, q0, Q_BLOCK + WINDOW, axis=1)
        vw = lax.dynamic_slice_in_dim(vw_pad, q0, Q_BLOCK + WINDOW, axis=1)
        kpos = q0 + win_offs
        d_w = t[:, None] - kpos[None]
        m_w = (d_w >= 0) & (d_w < WINDOW) & (kpos[None] >= 0)
        s_w = jnp.einsum('bqgrd,bkgd->bgrqk', qc, kw, preferred_element_type=jnp.float32) * scale \
            - slopes * d_w.astype(jnp.float32)
        p_w = masked_softmax(s_w, m_w)
        o_win = jnp.einsum('bgrqk,bkgd->bqgrd', p_w.astype(vw.dtype), vw)
        return gc[..., 0, None] * o_cmp + gc[..., 1, None] * o_slc + gc[..., 2, None] * o_win

    out = lax.map(chunk, jnp.arange(S // Q_BLOCK))
    return out.transpose(1, 0, 2, 3, 4, 5).reshape(B, S, ATTN_WIDTH)

def conv_module(a, b, w, bias, g, beta):
    u = a * jax.nn.sigmoid(b)
    y = lax.conv_general_dilated(u, w[:, None, :].astype(u.dtype), (1,), [(CONV_WIDTH - 1, 0)],
                                 dimension_numbers=('NWC', 'WIO', 'NWC'),
                                 feature_group_count=CONV_CH) + bias
    return jax.nn.silu(layer_norm(y, g, beta))

def setup_inputs(seed: int = 0) -> dict:
    key = jax.random.key(seed)
    ks = jax.random.split(key, 32)
    L, D, F = DEPTH, D_MODEL, D_FF

    def nrm(k, shape, scale):
        return jax.random.normal(k, shape, jnp.float32) * scale

    def gain(k, shape):
        return 1.0 + 0.02 * jax.random.normal(k, shape, jnp.float32)

    return {
        "x": nrm(ks[0], (BATCH, SEQ, D), 1.0),
        "ffn1_norm": gain(ks[1], (L, D)),
        "ffn1_w_gate": nrm(ks[2], (L, D, F), D ** -0.5),
        "ffn1_w_up": nrm(ks[3], (L, D, F), D ** -0.5),
        "ffn1_w_down": nrm(ks[4], (L, F, D), F ** -0.5),
        "mix_norm": gain(ks[5], (L, D)),
        "w_in": nrm(ks[6], (L, D, IN_WIDTH), D ** -0.5),
        "cmp_pos_k": nrm(ks[7], (L, CMP_BLOCK, HEAD_DIM), 0.02),
        "cmp_k_w1": nrm(ks[8], (L, CMP_BLOCK * HEAD_DIM, CMP_HIDDEN), (CMP_BLOCK * HEAD_DIM) ** -0.5),
        "cmp_k_w2": nrm(ks[9], (L, CMP_HIDDEN, HEAD_DIM), CMP_HIDDEN ** -0.5),
        "cmp_pos_v": nrm(ks[10], (L, CMP_BLOCK, HEAD_DIM), 0.02),
        "cmp_v_w1": nrm(ks[11], (L, CMP_BLOCK * HEAD_DIM, CMP_HIDDEN), (CMP_BLOCK * HEAD_DIM) ** -0.5),
        "cmp_v_w2": nrm(ks[12], (L, CMP_HIDDEN, HEAD_DIM), CMP_HIDDEN ** -0.5),
        "conv_w": nrm(ks[13], (L, CONV_WIDTH, CONV_CH), CONV_WIDTH ** -0.5),
        "conv_b": nrm(ks[14], (L, CONV_CH), 0.02),
        "conv_norm_g": gain(ks[15], (L, CONV_CH)),
        "conv_norm_b": nrm(ks[16], (L, CONV_CH), 0.02),
        "w_out": nrm(ks[17], (L, D, D), D ** -0.5),
        "ffn2_norm": gain(ks[18], (L, D)),
        "ffn2_w_gate": nrm(ks[19], (L, D, F), D ** -0.5),
        "ffn2_w_up": nrm(ks[20], (L, D, F), D ** -0.5),
        "ffn2_w_down": nrm(ks[21], (L, F, D), F ** -0.5),
        "final_norm": gain(ks[22], (D,)),
    }

def reference(x, ffn1_norm, ffn1_w_gate, ffn1_w_up, ffn1_w_down, mix_norm, w_in,
              cmp_pos_k, cmp_k_w1, cmp_k_w2, cmp_pos_v, cmp_v_w1, cmp_v_w2,
              conv_w, conv_b, conv_norm_g, conv_norm_b, w_out,
              ffn2_norm, ffn2_w_gate, ffn2_w_up, ffn2_w_down, final_norm):
    B, S = x.shape[0], x.shape[1]
    offsets = [int(v) for v in np.cumsum(SPLITS)[:-1]]
    for l in range(DEPTH):
        x = x + 0.5 * swiglu(rms_norm(x, ffn1_norm[l]), ffn1_w_gate[l], ffn1_w_up[l], ffn1_w_down[l])
        z = rms_norm(x, mix_norm[l]) @ w_in[l]
        q, kc, vc, ks_, vs_, kw, vw, gl, ga, gb = jnp.split(z, offsets, axis=-1)
        kv = lambda t: t.reshape(B, S, N_KV, HEAD_DIM)
        attn = nsa_attention(q, kv(kc), kv(vc), kv(ks_), kv(vs_), kv(kw), kv(vw), gl,
                             cmp_pos_k[l], cmp_k_w1[l], cmp_k_w2[l],
                             cmp_pos_v[l], cmp_v_w1[l], cmp_v_w2[l])
        conv = conv_module(ga, gb, conv_w[l], conv_b[l], conv_norm_g[l], conv_norm_b[l])
        x = x + jnp.concatenate([attn, conv], axis=-1) @ w_out[l]
        x = x + 0.5 * swiglu(rms_norm(x, ffn2_norm[l]), ffn2_w_gate[l], ffn2_w_up[l], ffn2_w_down[l])
    return rms_norm(x, final_norm)


_drawn_inputs = setup_inputs


def setup_inputs(seed=0):
    import zlib

    import numpy as np

    out = dict(_drawn_inputs(seed))
    spreads = {}
    factors = {'ffn1_norm': 4.539,
     'mix_norm': 3.734,
     'cmp_pos_k': 31.796,
     'cmp_pos_v': 41.551,
     'conv_norm_g': 21.02,
     'conv_norm_b': 21.821,
     'ffn2_norm': 5.711,
     'final_norm': 8.016,
     'conv_b': 8.0}
    for name, (base, spread) in spreads.items():
        noise = np.random.default_rng([zlib.crc32(name.encode()), seed]).standard_normal(out[name].shape)
        drawn = base * np.exp(spread * noise) if base else spread * noise
        out[name] = __import__('jax').numpy.asarray(drawn.astype(out[name].dtype))
    for name, factor in factors.items():
        out[name] = (out[name] * factor).astype(out[name].dtype)
    return out
```

```python
import concourse.bass as bass
from concourse import mybir

F32 = mybir.dt.float32
F32R = mybir.dt.float32r
ALU = mybir.AluOpType
ACT = mybir.ActivationFunctionType
AX = mybir.AxisListType

P = 128
D_MODEL, SEQ, DEPTH = 1024, 256, 2
N_HEADS, HEAD_DIM, N_KV = 8, 64, 2
GROUP = N_HEADS // N_KV
D_FF = 2816
CONV_CH, CONV_WIDTH = 512, 31
PAD = CONV_WIDTH - 1
CMP_BLOCK, CMP_STRIDE = 32, 16
NC = SEQ // CMP_STRIDE - 1
EPS = 1e-6
BIG = 3.0e38

KT = D_MODEL // P
QT = SEQ // P
CT = CONV_CH // P
FC = D_FF // P
BANK = 512
UNIT = 1024
RING = 6

FFN_UNITS = 3 * FC
U_GLU, U_KC, U_VC, U_KS, U_KW, U_Q, U_V, U_GATE, U_W1K, U_W1V, U_W2, U_OUT = 0, 8, 9, 10, 11, 12, 16, 18, 19, 23, 27, 28
MIX_UNITS = 36
MIX0 = FFN_UNITS
FFN2_0 = MIX0 + MIX_UNITS
LAYER_UNITS = FFN2_0 + FFN_UNITS
assert MIX0 % RING == 0 and FFN2_0 % RING == 0 and LAYER_UNITS % RING == 0

C_N1, C_NM, C_N2 = 0, KT, 2 * KT
C_CB = 3 * KT
C_CG = C_CB + CT
C_CBETA = C_CG + CT
C_CW = C_CBETA + CT
C_POS = C_CW + CONV_WIDTH * CT
LAYER_COLS = C_POS + 2 * (CMP_BLOCK // 2)

N_JOBS = 12
TAPS = CONV_WIDTH * CT


def unit_g(c):
    return 0 if c == 0 else 2 + 3 * (c - 1)


def unit_d(c):
    return FFN_UNITS - 1 if c == FC - 1 else unit_g(c + 1) + 2


def job(n):
    br, m = divmod(n, 6)
    if m < 4:
        return br, 1, [(m, 2), (m + GROUP, 2)]
    g = 2 * (m - 4)
    return br, 0, [(g, 1), (g + GROUP, 1), (g + 1, 1), (g + 1 + GROUP, 1)]


def trunk(nc, w, xT, params, bias, cbias, cmask, eye, out):
    from contextlib import ExitStack
    ctx = ExitStack()
    with ctx:
        sb = lambda name, shape, dt=F32: ctx.enter_context(nc.sbuf_tensor(name, shape, dt))
        sem = lambda name: ctx.enter_context(nc.semaphore(name))
        bank = ctx.enter_context(nc.psum_tensor("bank", [P, 8, BANK], F32))

        raw = sb("raw", [P, RING, UNIT])
        whi = sb("whi", [P, RING, UNIT], F32R)
        wlo = sb("wlo", [P, RING, UNIT], F32R)
        x = sb("x", [P, KT, SEQ])
        sq = sb("sq", [P, KT, SEQ])
        xn = sb("xn", [P, KT, SEQ])
        xh = sb("xh", [P, KT, SEQ], F32R)
        xl = sb("xl", [P, KT, SEQ], F32R)
        std = sb("std", [P, SEQ])
        rstd = sb("rstd", [P, SEQ])
        sil = sb("sil", [P, 2, SEQ])
        hid = sb("hid", [P, 2, SEQ])
        hh = sb("hh", [P, 2, SEQ], F32R)
        hl = sb("hl", [P, 2, SEQ], F32R)
        table = sb("table", [P, DEPTH * LAYER_COLS + KT])
        cur = sb("cur", [P, LAYER_COLS])
        alibi = sb("alibi", [P, N_HEADS, 2 * P])
        calibi = sb("calibi", [P, QT * N_HEADS * NC])
        cok = sb("cok", [P, QT * N_HEADS * NC])
        ident = sb("ident", [P, P])
        ones = sb("ones", [P, P])
        eps = sb("eps", [P, 1])
        sig = sb("sig", [P, 2, SEQ])
        upad = sb("upad", [P, CT, PAD + SEQ])
        y = sb("y", [P, CT, SEQ])
        mu = sb("mu", [P, SEQ])
        yc = sb("yc", [P, CT, SEQ])
        ysq = sb("ysq", [P, CT, SEQ])
        ystd = sb("ystd", [P, SEQ])
        yrstd = sb("yrstd", [P, SEQ])
        yn, cz = ysq, yc
        qT = sb("qT", [P, GROUP, SEQ])
        kz = sb("kz", [P, 2, N_KV, SEQ])
        v = sb("v", [P, QT, 2 * P])
        gT = sb("gT", [24, SEQ])
        gate = sb("gate", [P, QT, 24])
        kk = sb("kk", [P, 2, N_KV, SEQ])
        flat = sb("flat", [P, 2, CMP_BLOCK // 2, N_KV * NC])
        fh = sb("fh", [P, 2, CMP_BLOCK // 2, N_KV * NC], F32R)
        fl = sb("fl", [P, 2, CMP_BLOCK // 2, N_KV * NC], F32R)
        w2 = sb("w2", [P, 384])
        chid = sb("chid", [N_KV * NC, 2, 2 * P])
        chidT = sb("chidT", [P, 4 * N_KV * NC])
        kcz = sb("kcz", [P, N_KV, NC])
        vcd = sb("vcd", [P, N_KV, GROUP * HEAD_DIM])
        cs = sb("cs", [P, QT * N_HEADS, NC])
        cmx = sb("cmx", [P, QT * N_HEADS])
        ce = sb("ce", [P, QT * N_HEADS, NC])
        csum = sb("csum", [P, QT * N_HEADS])
        cp = sb("cp", [P, QT, N_KV, GROUP, 32])
        cpT = sb("cpT", [P, QT, N_KV, P])
        ch, ah = xh[:, 0:CT, :], xh[:, CT:KT, :]
        cl, al = xl[:, 0:CT, :], xl[:, CT:KT, :]
        pr = xn[:, 0:4, :].rearrange("p (b a) t -> p b (a t)", b=2)
        held = sb("held", [P, 2])
        nmax = sb("nmax", [P, 2, 4])
        prT = xn[:, 4:8, :].rearrange("p (b a) t -> p b (a t)", b=2)
        rsum = sb("rsum", [P, 2, QT, N_HEADS])
        rrec = sb("rrec", [P, 3, QT, N_HEADS])
        fac = sb("fac", [P, 3, QT, N_HEADS])
        oacc = sb("oacc", [P, QT, BANK])
        otmp = sq[:].rearrange("p (b t a) s -> p b t (a s)", b=2, t=QT)

        landed = [sem(f"landed{s}") for s in range(RING)]
        consts_in, x_in, out_done = sem("consts_in"), sem("x_in"), sem("out_done")
        setup_done = sem("setup_done")
        cur_ready = sem("cur_ready")
        hi_ready, lo_ready, unit_used = sem("hi_ready"), sem("lo_ready"), sem("unit_used")
        x_ready, sq_ready, ssum_ready = sem("x_ready"), sem("sq_ready"), sem("ssum_ready")
        std_ready, rstd_ready = sem("std_ready"), sem("rstd_ready")
        xn_ready, xh_ready, xl_ready = sem("xn_ready"), sem("xh_ready"), sem("xl_ready")
        y_ready = sem("y_ready")
        sil_ready, hid_ready, hh_ready, hl_ready = sem("sil_ready"), sem("hid_ready"), sem("hh_ready"), sem("hl_ready")
        sig_ready, glu_ready, tap_done = sem("sig_ready"), sem("glu_ready"), sem("tap_done")
        ysum_ready, mu_ready, yc_ready, ysq_ready = sem("ysum_ready"), sem("mu_ready"), sem("yc_ready"), sem("ysq_ready")
        yvar_ready, ystd_ready, yrstd_ready, yn_ready = sem("yvar_ready"), sem("ystd_ready"), sem("yrstd_ready"), sem("yn_ready")
        cz_ready, ch_ready, cl_ready = sem("cz_ready"), sem("ch_ready"), sem("cl_ready")
        kk_ready, kz_ready, q_ready, v_ready = sem("kk_ready"), sem("kz_ready"), sem("q_ready"), sem("v_ready")
        gT_ready, gate_turned, gate_ready = sem("gT_ready"), sem("gate_turned"), sem("gate_ready")
        flat_ready, fh_ready, fl_ready = sem("flat_ready"), sem("fh_ready"), sem("fl_ready")
        w2_ready, chid_ready, chid_turned, chidT_ready = sem("w2_ready"), sem("chid_ready"), sem("chid_turned"), sem("chidT_ready")
        cmpkv_done, cmpkv_ready, cscore_done = sem("cmpkv_done"), sem("cmpkv_ready"), sem("cscore_done")
        cs_step, ce_ready, cp_ready, cp_turned, cpT_ready, cpv_done = (
            sem("cs_step"), sem("ce_ready"), sem("cp_ready"), sem("cp_turned"), sem("cpT_ready"), sem("cpv_done"))
        scores_done, scored, probs, turned, prT_ready, pv_done = (
            sem("scores_done"), sem("scored"), sem("probs"), sem("turned"), sem("prT_ready"), sem("pv_done"))
        fac_step, o_step, o_turned, ah_ready, al_ready = (
            sem("fac_step"), sem("o_step"), sem("o_turned"), sem("ah_ready"), sem("al_ready"))

        block = ctx.enter_context(nc.Block())
        f32 = lambda ap: ap.bitcast(F32)

        @block.sync
        def _(sp):
            sp.dma_start(xn[:], xT).then_inc(x_in, 16)
            for s in range(RING):
                sp.dma_start(raw[:, s, :], w[s]).then_inc(landed[s], 16)
            sp.dma_start(table[:], params).then_inc(consts_in, 16)
            sp.dma_start(ident[:], eye).then_inc(consts_in, 16)
            sp.dma_start(alibi[:], bias).then_inc(consts_in, 16)
            sp.dma_start(calibi[:], cbias).then_inc(consts_in, 16)
            sp.dma_start(cok[:], cmask).then_inc(consts_in, 16)
            with sp.Fori(1, DEPTH * LAYER_UNITS // RING) as r:
                for s in range(RING):
                    sp.wait_ge(lo_ready, r * RING + (s - RING + 1))
                    sp.dma_start(raw[:, s, :], w[r * RING + s]).then_inc(landed[s], 16)
            for k in range(KT):
                sp.wait_ge(xn_ready, 3 * DEPTH * KT + k + 1)
                sp.dma_start(out[:, k, :], xn[:, k, :]).then_inc(out_done, 16)
            sp.wait_ge(out_done, 16 * KT)

        @block.gpsimd
        def _(pool):
            nc.gpsimd.memset(upad[:, :, 0:PAD], 0.0).then_inc(setup_done, 1)
            nc.gpsimd.memset(kz[:], 0.0).then_inc(setup_done, 1)
            nc.gpsimd.memset(kcz[:], 0.0).then_inc(setup_done, 1)
            nc.gpsimd.memset(vcd[:], 0.0).then_inc(setup_done, 1)
            nc.gpsimd.memset(cp[:], 0.0).then_inc(setup_done, 1)
            nc.gpsimd.memset(ones[:], 1.0).then_inc(setup_done, 1)
            nc.gpsimd.memset(eps[:], EPS).then_inc(setup_done, 1)

        SETUP = 7

        @block.scalar
        def _(act):
            def hi(l, n):
                act.wait_ge(landed[n % RING], l * (16 * LAYER_UNITS // RING) + 16 * (n // RING + 1))
                if n >= RING:
                    act.wait_ge(unit_used, l * LAYER_UNITS + (n - RING + 1))
                nc.scalar.copy(whi[:, n % RING, :], raw[:, n % RING, :]).then_inc(hi_ready, 1)

            def hi_in_loop(l, j, n):
                act.wait_ge(landed[n % RING], l * (16 * LAYER_UNITS // RING) + j * 16 + 16 * (n // RING + 1))
                act.wait_ge(unit_used, l * LAYER_UNITS + j * RING + (n - RING + 1))
                nc.scalar.copy(whi[:, n % RING, :], raw[:, n % RING, :]).then_inc(hi_ready, 1)

            def squares(q4):
                for b in range(4):
                    act.wait_ge(x_ready, q4 + (b + 1))
                    nc.scalar.activation(sq[:, 2 * b:2 * b + 2, :], x[:, 2 * b:2 * b + 2, :], ACT.Square).then_inc(sq_ready, 1)

            def root(q):
                act.wait_ge(ssum_ready, q + 1)
                nc.scalar.activation(std[:], bank[:, 7, 0:SEQ], ACT.Sqrt, scale=1.0 / D_MODEL,
                                     bias=eps[:, 0:1]).then_inc(std_ready, 1)

            def high_x(q8):
                for k in range(KT):
                    act.wait_ge(xn_ready, q8 + (k + 1))
                    nc.scalar.copy(xh[:, k, :], xn[:, k, :]).then_inc(xh_ready, 1)

            def silu(l, ffn, j, c):
                act.wait_ge(unit_used, l * LAYER_UNITS + j * RING + ((FFN2_0 if ffn else 0) + unit_g(c) + 1))
                nc.scalar.activation(sil[:, c % 2, :], bank[:, 4 + 2 * (c % 2), 0:SEQ], ACT.Silu).then_inc(sil_ready, 1)

            def ffn(l, f):
                base = FFN2_0 if f else 0
                last = LAYER_UNITS
                for c in (0, 1):
                    silu(l, f, 0, c)
                    for n in range(unit_g(c), unit_g(c + 1)):
                        hi(l, base + n + RING)
                with act.Fori(0, (FC - 4) // 2) as j:
                    for c in (2, 3):
                        silu(l, f, j, c)
                        for n in range(unit_g(c), unit_g(c + 1)):
                            hi_in_loop(l, j, base + n + RING)
                for c in (FC - 2, FC - 1):
                    silu(l, f, 0, c)
                    for n in range(unit_g(c), min(unit_g(c) + 3, FFN_UNITS - 1)):
                        if base + n + RING < last:
                            hi(l, base + n + RING)

            act.wait_ge(setup_done, SETUP)
            with act.Fori(0, DEPTH) as l:
                squares(l * 12)
                for n in range(3):
                    hi(l, n)
                root(l * 3)
                high_x(l * 24)
                for n in range(3, RING):
                    hi(l, n)
                ffn(l, 0)

                squares(l * 12 + 4)
                hi(l, MIX0 - 1 + RING)
                root(l * 3 + 1)
                high_x(l * 24 + 8)

                def done(u):
                    act.wait_ge(unit_used, l * LAYER_UNITS + (MIX0 + u + 1))

                for u in range(U_OUT):
                    done(u)
                    if u < U_KC and u % 2 == 0:
                        t = u // 2 % 2
                        nc.scalar.activation(sig[:, t, :], bank[:, 4 + 2 * t, 0:SEQ], ACT.Sigmoid).then_inc(sig_ready, 1)
                    if u in (U_KC, U_VC):
                        i = u - U_KC
                        for kv in range(N_KV):
                            src = bank[64 * kv:64 * kv + 64, 4 + i, :]
                            nc.scalar.copy(kk[0:64, i, kv, :], src[:, 0:SEQ]).then_inc(kk_ready, 1)
                            nc.scalar.copy(kk[64:128, i, kv, 0:SEQ - 1], src[:, 1:SEQ]).then_inc(kk_ready, 1)
                    if u in (U_KS, U_KW):
                        i = u - U_KS
                        for kv in range(N_KV):
                            r = slice(64 * kv, 64 * kv + 64)
                            nc.scalar.copy(kz[r, i, kv, :], bank[r, 6 + i, 0:SEQ]).then_inc(kz_ready, 1)
                    if U_Q <= u < U_V:
                        nc.scalar.copy(qT[:, u - U_Q, :], bank[:, u - U_Q, 0:SEQ]).then_inc(q_ready, 1)
                    if u == U_V + 1:
                        for t in range(QT):
                            nc.scalar.copy(v[:, t, :], bank[:, 4 + t, 0:SEQ]).then_inc(v_ready, 1)
                    if u == U_GATE:
                        nc.scalar.activation(gT[:], bank[0:24, 6, 0:SEQ], ACT.Sigmoid).then_inc(gT_ready, 1)
                    if u in (U_W1K + 3, U_W1V + 3):
                        i = (u - U_W1K) // 4
                        nc.scalar.activation(chid[:, i, :], bank[0:N_KV * NC, 4 + i, 0:2 * P], ACT.Silu).then_inc(chid_ready, 1)
                    hi(l, MIX0 + u + RING)

                def exps(n):
                    br, qt, segs = job(n)
                    act.wait_ge(scored, l * N_JOBS + (n + 1))
                    at = 0
                    for i, (h, kb) in enumerate(segs):
                        p = pr[:, n % 2, at:at + P * kb]
                        e = nc.scalar.activation(p, p, ACT.Exp, scale=-1.0, bias=nmax[:, n % 2, i:i + 1],
                                                 accum_out=rsum[:, br, qt, h:h + 1])
                        at += P * kb
                    e.then_inc(probs, 1)

                act.wait_ge(cs_step, l * 5 + 3)
                nc.scalar.activation(ce[:], cs[:], ACT.Exp).then_inc(ce_ready, 1)
                exps(0)
                exps(1)
                act.wait_ge(yc_ready, l + 1)
                nc.scalar.activation(ysq[:], yc[:], ACT.Square).then_inc(ysq_ready, 1)
                for n in range(2, N_JOBS):
                    exps(n)
                    if n == 4:
                        act.wait_ge(yvar_ready, l + 1)
                        nc.scalar.activation(ystd[:], bank[:, 3, 0:SEQ], ACT.Sqrt, scale=1.0 / CONV_CH,
                                             bias=eps[:, 0:1]).then_inc(ystd_ready, 1)
                act.wait_ge(yn_ready, l + 1)
                for t in range(CT):
                    nc.scalar.activation(cz[:, t, :], yn[:, t, :], ACT.Silu, scale=cur[:, C_CG + t:C_CG + t + 1],
                                         bias=cur[:, C_CBETA + t:C_CBETA + t + 1]).then_inc(cz_ready, 1)
                act.wait_ge(cz_ready, l * CT + CT)
                nc.scalar.copy(ch, cz[:]).then_inc(ch_ready, 1)
                for u in range(U_OUT, U_OUT + 4):
                    hi(l, MIX0 + u + RING)
                act.wait_ge(o_turned, l + 1)
                for b in range(2):
                    nc.scalar.copy(ah[:, 2 * b:2 * b + 2, :], bank[:, 6 + b, :]).then_inc(ah_ready, 1)
                for u in range(U_OUT + 4, MIX_UNITS - 1):
                    hi(l, MIX0 + u + RING)

                squares(l * 12 + 8)
                hi(l, FFN2_0 - 1 + RING)
                root(l * 3 + 2)
                high_x(l * 24 + 16)
                ffn(l, 1)
            squares(DEPTH * 12)
            root(DEPTH * 3)

        @block.vector
        def _(dve):
            def lo(l, n):
                dve.wait_ge(hi_ready, l * LAYER_UNITS + (n + 1))
                nc.vector.tensor_tensor(wlo[:, n % RING, :], raw[:, n % RING, :], f32(whi[:, n % RING, :]),
                                        ALU.subtract).then_inc(lo_ready, 1)

            def lo_in_loop(l, j, n):
                dve.wait_ge(hi_ready, l * LAYER_UNITS + j * RING + (n + 1))
                nc.vector.tensor_tensor(wlo[:, n % RING, :], raw[:, n % RING, :], f32(whi[:, n % RING, :]),
                                        ALU.subtract).then_inc(lo_ready, 1)

            def residual(y4, scale):
                for b in range(4):
                    dve.wait_ge(y_ready, y4 + (b + 1))
                    xb = x[:, 2 * b:2 * b + 2, :].rearrange("p a t -> p (a t)")
                    nc.vector.scalar_tensor_tensor(out=xb, in0=bank[:, b, :], scalar=scale, in1=xb,
                                                   op0=ALU.mult, op1=ALU.add).then_inc(x_ready, 1)

            def recip(q):
                dve.wait_ge(std_ready, q + 1)
                nc.vector.reciprocal(rstd[:], std[:]).then_inc(rstd_ready, 1)
                dve.wait_ge(rstd_ready, q + 1)

            def normed(k, gains):
                nc.vector.scalar_tensor_tensor(out=xn[:, k, :], in0=x[:, k, :], scalar=gains[:, k:k + 1],
                                               in1=rstd[:], op0=ALU.mult, op1=ALU.mult).then_inc(xn_ready, 1)

            def low_x(q8, k):
                dve.wait_ge(xh_ready, q8 + (k + 1))
                nc.vector.tensor_tensor(xl[:, k, :], xn[:, k, :], f32(xh[:, k, :]), ALU.subtract).then_inc(xl_ready, 1)

            def norm(q, q8, gains):
                recip(q)
                for k in range(KT + 1):
                    if k < KT:
                        normed(k, gains)
                    if k:
                        low_x(q8, k - 1)

            def hidden(l, f, j, c):
                h0 = f * FC + c + 1
                dve.wait_ge(sil_ready, l * 2 * FC + j * 2 + h0)
                dve.wait_ge(unit_used, l * LAYER_UNITS + j * RING + ((FFN2_0 if f else 0) + unit_g(c) + 2))
                b = c % 2
                nc.vector.tensor_tensor(hid[:, b, :], bank[:, 5 + 2 * b, 0:SEQ], sil[:, b, :], ALU.mult).then_inc(hid_ready, 1)
                dve.wait_ge(hid_ready, l * 2 * FC + j * 2 + h0)
                nc.vector.tensor_copy(hh[:, b, :], hid[:, b, :]).then_inc(hh_ready, 1)
                dve.wait_ge(hh_ready, l * 2 * FC + j * 2 + h0)
                nc.vector.tensor_tensor(hl[:, b, :], hid[:, b, :], f32(hh[:, b, :]), ALU.subtract).then_inc(hl_ready, 1)

            def ffn(l, f):
                base = FFN2_0 if f else 0
                for c in (0, 1):
                    lo(l, base + unit_g(c) + RING)
                    hidden(l, f, 0, c)
                    for n in range(unit_g(c) + 1, unit_g(c + 1)):
                        lo(l, base + n + RING)
                with dve.Fori(0, (FC - 4) // 2) as j:
                    for c in (2, 3):
                        lo_in_loop(l, j, base + unit_g(c) + RING)
                        hidden(l, f, j, c)
                        for n in range(unit_g(c) + 1, unit_g(c + 1)):
                            lo_in_loop(l, j, base + n + RING)
                for c in (FC - 2, FC - 1):
                    for i, n in enumerate(range(unit_g(c), min(unit_g(c) + 3, FFN_UNITS - 1))):
                        if i == 1:
                            hidden(l, f, 0, c)
                        if base + n + RING < LAYER_UNITS:
                            lo(l, base + n + RING)

            dve.wait_ge(setup_done, SETUP)
            dve.wait_ge(x_in, 16)
            for b in range(4):
                nc.vector.tensor_copy(x[:, 2 * b:2 * b + 2, :], xn[:, 2 * b:2 * b + 2, :]).then_inc(x_ready, 1)
            dve.wait_ge(consts_in, 16 * 5)
            with dve.Fori(0, DEPTH) as l:
                nc.vector.tensor_copy(cur[:], table[:, bass.ds(l * LAYER_COLS, LAYER_COLS)]).then_inc(cur_ready, 1)
                for n in range(3):
                    lo(l, n)
                dve.wait_ge(cur_ready, l + 1)
                norm(l * 3, l * 24, cur[:, C_N1:C_N1 + KT])
                for n in range(3, RING):
                    lo(l, n)
                ffn(l, 0)
                residual(l * 12, 0.5)

                lo(l, MIX0 - 1 + RING)
                norm(l * 3 + 1, l * 24 + 8, cur[:, C_NM:C_NM + KT])

                def done(u):
                    dve.wait_ge(unit_used, l * LAYER_UNITS + (MIX0 + u + 1))

                def tap(i):
                    j, t = divmod(i, CT)
                    wj = cur[:, C_CW + i:C_CW + i + 1]
                    src = upad[:, t, j:j + SEQ]
                    if j == 0:
                        nc.vector.tensor_scalar(y[:, t, :], src, wj, cur[:, C_CB + t:C_CB + t + 1],
                                                ALU.mult, ALU.add).then_inc(tap_done, 1)
                    else:
                        dve.wait_ge(tap_done, l * TAPS + (i - CT + 1))
                        nc.vector.scalar_tensor_tensor(out=y[:, t, :], in0=src, scalar=wj, in1=y[:, t, :],
                                                       op0=ALU.mult, op1=ALU.add).then_inc(tap_done, 1)

                next_tap = 0
                for u in range(U_OUT):
                    if u < U_KC and u % 2 == 1:
                        t = u // 2
                        done(u)
                        dve.wait_ge(sig_ready, l * CT + (t + 1))
                        nc.vector.tensor_tensor(upad[:, t, PAD:PAD + SEQ], bank[:, 5 + 2 * (t % 2), 0:SEQ],
                                                sig[:, t % 2, :], ALU.mult).then_inc(glu_ready, 1)
                    if u == U_KC:
                        dve.wait_ge(glu_ready, l * CT + CT)
                    if u in (U_VC + 2, U_VC + 3):
                        i = u - U_VC - 2
                        dve.wait_ge(kk_ready, l * 8 + 4 * i + 4)
                        for kv in range(N_KV):
                            src = bass.AP if False else kk[:, i, kv, :].rearrange("p (n s) -> p s n", s=CMP_STRIDE)
                            for half in range(2):
                                a = src[:, 0:CMP_STRIDE:2, half:half + NC]
                                pos = cur[:, C_POS + 16 * i + 8 * half:C_POS + 16 * i + 8 * half + 8]
                                nc.vector.tensor_tensor(
                                    flat[:, i, 8 * half:8 * half + 8, kv * NC:(kv + 1) * NC], a,
                                    pos.rearrange("p (j o) -> p j o", o=1).to_broadcast([P, 8, NC]), ALU.add).then_inc(flat_ready, 1)
                        dve.wait_ge(flat_ready, l * 8 + 4 * i + 4)
                        nc.vector.tensor_copy(fh[:, i], flat[:, i]).then_inc(fh_ready, 1)
                        dve.wait_ge(fh_ready, l * 2 + i + 1)
                        nc.vector.tensor_tensor(fl[:, i], flat[:, i], f32(fh[:, i]), ALU.subtract).then_inc(fl_ready, 1)
                    if u == U_GATE + 1:
                        dve.wait_ge(gate_turned, l + 1)
                        nc.vector.tensor_copy(gate[:], bank[:, 7, 0:QT * 24].rearrange("p (t g) -> p t g", t=QT)).then_inc(gate_ready, 1)
                    if u + RING == U_W2:
                        dve.wait_ge(landed[(MIX0 + U_W2) % RING], l * (16 * LAYER_UNITS // RING) + 16 * ((MIX0 + U_W2) // RING + 1))
                        nc.vector.tensor_copy(w2[:], raw[:, (MIX0 + U_W2) % RING, 0:384]).then_inc(w2_ready, 1)
                    if u < U_OUT - 1:
                        lo(l, MIX0 + u + RING)
                    if u >= U_KC:
                        n_taps = 10 if u == U_KC else 6
                        for i in range(next_tap, min(next_tap + n_taps, TAPS)):
                            tap(i)
                        next_tap = min(next_tap + n_taps, TAPS)
                for i in range(next_tap, TAPS):
                    tap(i)
                dve.wait_ge(chid_turned, l + 1)
                nc.vector.tensor_copy(chidT[:], bank[:, 6, 0:4 * N_KV * NC]).then_inc(chidT_ready, 1)
                lo(l, MIX0 + U_OUT - 1 + RING)
                dve.wait_ge(cmpkv_done, l + 1)
                for kv in range(N_KV):
                    r = slice(64 * kv, 64 * kv + 64)
                    nc.vector.tensor_copy(kcz[r, kv, :], bank[r, 7, kv * NC:(kv + 1) * NC]).then_inc(cmpkv_ready, 1)
                for kv in range(N_KV):
                    for g in range(GROUP):
                        nc.vector.tensor_copy(vcd[32 * g:32 * g + NC, kv, g * HEAD_DIM:(g + 1) * HEAD_DIM],
                                              bank[0:NC, 7, 64 + 64 * kv:128 + 64 * kv]).then_inc(cmpkv_ready, 1)

                dve.wait_ge(cscore_done, l + 1)
                csf = cs[:].rearrange("p a n -> p (a n)")
                nc.vector.scalar_tensor_tensor(out=csf, in0=bank[:, 6, 0:QT * N_HEADS * NC], scalar=HEAD_DIM ** -0.5,
                                               in1=calibi[:], op0=ALU.mult, op1=ALU.add).then_inc(cs_step, 1)
                dve.wait_ge(cs_step, l * 5 + 1)
                nc.vector.tensor_reduce(cmx[:], cs[:], AX.X, ALU.max).then_inc(cs_step, 1)
                dve.wait_ge(cs_step, l * 5 + 2)
                nc.vector.tensor_tensor(cs[:], cs[:], cmx[:].rearrange("p (a o) -> p a o", o=1).to_broadcast([P, QT * N_HEADS, NC]),
                                        ALU.subtract).then_inc(cs_step, 1)

                def score(n):
                    br, qt, segs = job(n)
                    dve.wait_ge(scores_done, l * N_JOBS + (n + 1))
                    if n >= 2:
                        dve.wait_ge(turned, l * N_JOBS + (n - 1))
                    nc.vector.memset(held[:, n % 2:n % 2 + 1], 0.0)
                    at = 0
                    for i, (h, kb) in enumerate(segs):
                        s = nc.vector.tensor_tensor_reduce(
                            pr[:, n % 2, at:at + P * kb], bank[:, 4 + n % 2, at:at + P * kb], alibi[:, h, 2 * P - P * kb:],
                            -(HEAD_DIM ** -0.5), BIG, ALU.add, ALU.min, nmax[:, n % 2, i:i + 1])
                        at += P * kb
                    s.then_inc(scored, 1)

                def copy_prT(n):
                    dve.wait_ge(turned, l * N_JOBS + (n + 1))
                    if n >= 2:
                        dve.wait_ge(pv_done, l * N_JOBS + (n - 1))
                    nc.vector.tensor_copy(prT[:, n % 2, :], bank[:, 6 + n % 2, :]).then_inc(prT_ready, 1)

                def factors(b, sums, gates, k0):
                    nc.vector.reciprocal(rrec[:, b], sums).then_inc(fac_step, 1)
                    dve.wait_ge(fac_step, l * 6 + k0 + 1)
                    nc.vector.tensor_tensor(fac[:, b], rrec[:, b], gates, ALU.mult).then_inc(fac_step, 1)
                    dve.wait_ge(fac_step, l * 6 + k0 + 2)

                def weigh(dst, src, b, qt):
                    nc.vector.tensor_tensor(
                        dst.rearrange("p (h d) -> p h d", h=N_HEADS), src.rearrange("p (h d) -> p h d", h=N_HEADS),
                        fac[:, b, qt, :].rearrange("p (h o) -> p h o", o=1).to_broadcast([P, N_HEADS, HEAD_DIM]),
                        ALU.mult).then_inc(o_step, 1)

                score(0)
                score(1)
                dve.wait_ge(ysum_ready, l + 1)
                nc.vector.tensor_scalar(mu[:], bank[:, 2, 0:SEQ], 1.0 / CONV_CH, None, ALU.mult).then_inc(mu_ready, 1)
                dve.wait_ge(mu_ready, l + 1)
                nc.vector.tensor_tensor(yc[:], y[:], mu[:].rearrange("p (o t) -> p o t", o=1).to_broadcast([P, CT, SEQ]),
                                        ALU.subtract).then_inc(yc_ready, 1)
                dve.wait_ge(ce_ready, l + 1)
                nc.vector.tensor_reduce(csum[:], ce[:], AX.X, ALU.add).then_inc(cs_step, 1)
                for qt in range(QT):
                    o = cp[:, qt].rearrange("p kv c n -> p c kv n")[:, :, :, 0:NC]
                    m = cok[:].rearrange("p (t c kv n) -> p t c kv n", t=QT, c=GROUP, kv=N_KV)[:, qt]
                    e = ce[:].rearrange("p (t c kv) n -> p t c kv n", t=QT, c=GROUP)[:, qt]
                    nc.vector.tensor_tensor(o, e, m, ALU.mult).then_inc(cp_ready, 1)
                for n in range(N_JOBS):
                    copy_prT(n)
                    if n + 2 < N_JOBS:
                        score(n + 2)
                    if n == 5:
                        dve.wait_ge(ystd_ready, l + 1)
                        nc.vector.reciprocal(yrstd[:], ystd[:]).then_inc(yrstd_ready, 1)
                    if n == 6:
                        dve.wait_ge(yrstd_ready, l + 1)
                        nc.vector.tensor_tensor(yn[:], yc[:], yrstd[:].rearrange("p (o t) -> p o t", o=1).to_broadcast([P, CT, SEQ]),
                                                ALU.mult).then_inc(yn_ready, 1)
                    if n == 7:
                        dve.wait_ge(gate_ready, l + 1)
                        dve.wait_ge(probs, l * N_JOBS + 6)
                        gsel = gate[:].rearrange("p t (b h) -> p t b h", b=3)
                        factors(1, rsum[:, 0], gsel[:, :, 1, :], 0)
                        dve.wait_ge(pv_done, l * N_JOBS + 6)
                        for qt in range(QT):
                            weigh(oacc[:, qt, :], bank[:, qt, :], 1, qt)
                dve.wait_ge(probs, l * N_JOBS + 12)
                factors(2, rsum[:, 1], gsel[:, :, 2, :], 2)
                dve.wait_ge(cs_step, l * 5 + 4)
                nc.vector.tensor_copy(cmx[:].rearrange("p (t kv c) -> p t kv c", t=QT, kv=N_KV),
                                      csum[:].rearrange("p (t c kv) -> p t kv c", t=QT, kv=N_KV)).then_inc(cs_step, 1)
                dve.wait_ge(cs_step, l * 5 + 5)
                factors(0, cmx[:].rearrange("p (t h) -> p t h", t=QT), gsel[:, :, 0, :], 4)
                dve.wait_ge(cp_turned, l + 1)
                nc.vector.tensor_copy(cpT[:].rearrange("p t k q -> p (t k q)"), bank[:, 6, :]).then_inc(cpT_ready, 1)
                dve.wait_ge(pv_done, l * N_JOBS + 12)
                for qt in range(QT):
                    weigh(otmp[:, 0, qt, :], bank[:, 2 + qt, :], 2, qt)
                dve.wait_ge(ch_ready, l + 1)
                nc.vector.tensor_tensor(cl, cz[:], f32(ch), ALU.subtract).then_inc(cl_ready, 1)
                dve.wait_ge(cpv_done, l + 1)
                for qt in range(QT):
                    weigh(otmp[:, 1, qt, :], bank[:, 4 + qt, :], 0, qt)
                dve.wait_ge(o_step, l * 8 + 4)
                nc.vector.tensor_tensor(oacc[:], oacc[:], otmp[:, 0], ALU.add).then_inc(o_step, 1)
                dve.wait_ge(o_step, l * 8 + 7)
                nc.vector.tensor_tensor(oacc[:], oacc[:], otmp[:, 1], ALU.add).then_inc(o_step, 1)
                for u in range(U_OUT, U_OUT + 2):
                    lo(l, MIX0 + u + RING)
                for b in range(2):
                    dve.wait_ge(ah_ready, l * 2 + b + 1)
                    nc.vector.tensor_tensor(al[:, 2 * b:2 * b + 2, :].rearrange("p a t -> p (a t)"), bank[:, 6 + b, :],
                                            f32(ah[:, 2 * b:2 * b + 2, :]).rearrange("p a t -> p (a t)"),
                                            ALU.subtract).then_inc(al_ready, 1)
                for u in range(U_OUT + 2, MIX_UNITS - 1):
                    lo(l, MIX0 + u + RING)
                residual(l * 12 + 4, 1.0)

                lo(l, FFN2_0 - 1 + RING)
                norm(l * 3 + 2, l * 24 + 16, cur[:, C_N2:C_N2 + KT])
                ffn(l, 1)
                residual(l * 12 + 8, 0.5)
            recip(DEPTH * 3)
            for k in range(KT):
                normed(k, table[:, DEPTH * LAYER_COLS:])

        @block.tensor
        def _(pe):
            mm = nc.tensor.matmul

            def parts(o, n, col, width, a_hi, a_lo, start, stop, more=False):
                s = n % RING
                wh, wl = whi[:, s, col:col + width], wlo[:, s, col:col + width]
                mm(o, wh, a_hi, start=start, stop=False, skip_group_check=more)
                mm(o, wh, a_lo, start=False, stop=False, skip_group_check=more)
                return mm(o, wl, a_hi, start=False, stop=stop, skip_group_check=more)

            def sum_squares(q, q4):
                for b in range(4):
                    pe.wait_ge(sq_ready, q4 + (b + 1))
                    for k in (2 * b, 2 * b + 1):
                        m = mm(bank[:, 7, 0:SEQ], ones[:], sq[:, k, :], start=(k == 0), stop=(k == KT - 1))
                m.then_inc(ssum_ready, 1)

            def split(at):
                pe.wait_ge(lo_ready, at)

            def project(n, o, width=P, x_from=None):
                for k in range(KT):
                    if x_from is not None:
                        pe.wait_ge(xl_ready, x_from + (k + 1))
                    m = parts(o, n, k * width, width, xh[:, k, :], xl[:, k, :], k == 0, k == KT - 1)
                m.then_inc(unit_used, 1)

            def to_residual(n, a_hi, a_lo, first, last):
                for m8 in range(KT):
                    m = parts(bank[:, m8 // 2, (m8 % 2) * SEQ:(m8 % 2 + 1) * SEQ], n, m8 * P, P, a_hi, a_lo,
                              first and m8 % 2 == 0, last, more=True)
                    if last and m8 % 2 == 1:
                        if m8 == KT - 1:
                            m.then_inc(y_ready, 1)
                        else:
                            m.then_inc(y_ready, 1)
                return m

            def ffn(l, f, x8):
                base = FFN2_0 if f else 0
                L = LAYER_UNITS

                def gate_up(c, j=None):
                    n, b = base + unit_g(c), 4 + 2 * (c % 2)
                    at, ht = l * L + n, l * 2 * FC + (f * FC + c - 1)
                    if j is not None:
                        at, ht = at + j * RING, ht + j * 2
                    if c >= 2:
                        pe.wait_ge(hid_ready, ht)
                    split(at + 1)
                    project(n, bank[:, b, 0:SEQ], x_from=x8 if c == 0 else None)
                    split(at + 2)
                    project(n + 1, bank[:, b + 1, 0:SEQ])

                def down(c, j=None):
                    n = base + unit_d(c)
                    at, ht = l * L + n, l * 2 * FC + (f * FC + c + 1)
                    if j is not None:
                        at, ht = at + j * RING, ht + j * 2
                    pe.wait_ge(hl_ready, ht)
                    split(at + 1)
                    m = to_residual(n, hh[:, c % 2, :], hl[:, c % 2, :], c == 0, c == FC - 1)
                    if c < FC - 1:
                        m.then_inc(unit_used, 1)

                gate_up(0)
                gate_up(1)
                down(0)
                with pe.Fori(0, (FC - 4) // 2) as j:
                    for c in (2, 3):
                        gate_up(c, j)
                        down(c - 1, j)
                gate_up(FC - 2)
                down(FC - 3)
                gate_up(FC - 1)
                down(FC - 2)
                down(FC - 1)
                last_unit()

            def last_unit():
                mm(bank[0:1, 6, 0:1], ones[:, 0:1], ones[:, 0:1], start=True, stop=True).then_inc(unit_used, 1)

            pe.wait_ge(setup_done, SETUP)
            pe.wait_ge(consts_in, 16 * 5)
            with pe.Fori(0, DEPTH) as l:
                sum_squares(l * 3, l * 12)
                ffn(l, 0, l * 24)
                sum_squares(l * 3 + 1, l * 12 + 4)

                def used(u):
                    split(l * LAYER_UNITS + (MIX0 + u + 1))

                for t in range(CT):
                    if t >= 2:
                        pe.wait_ge(glu_ready, l * CT + (t - 1))
                    for i in range(2):
                        used(2 * t + i)
                        project(MIX0 + 2 * t + i, bank[:, 4 + 2 * (t % 2) + i, 0:SEQ],
                                x_from=l * 24 + 8 if t == 0 and i == 0 else None)
                pe.wait_ge(glu_ready, l * CT + 3)
                for i in range(2):
                    used(U_KC + i)
                    project(MIX0 + U_KC + i, bank[:, 4 + i, 0:SEQ])
                pe.wait_ge(glu_ready, l * CT + 4)
                for i in range(2):
                    used(U_KS + i)
                    project(MIX0 + U_KS + i, bank[:, 6 + i, 0:SEQ])
                for c in range(GROUP):
                    used(U_Q + c)
                    project(MIX0 + U_Q + c, bank[:, c, 0:SEQ])
                pe.wait_ge(kk_ready, l * 8 + 8)
                for i in range(2):
                    used(U_V + i)
                    s = (MIX0 + U_V + i) % RING
                    for k4 in range(4):
                        k = 4 * i + k4
                        for t in range(QT):
                            xs = slice(t * P, (t + 1) * P)
                            wv = slice(k4 * 2 * P, (k4 + 1) * 2 * P)
                            o = bank[:, 4 + t, 0:2 * P]
                            mm(o, xh[:, k, xs], whi[:, s, wv], start=(k == 0), stop=False)
                            mm(o, xl[:, k, xs], whi[:, s, wv], start=False, stop=False)
                            m = mm(o, xh[:, k, xs], wlo[:, s, wv], start=False, stop=(k == KT - 1))
                    m.then_inc(unit_used, 1)
                pe.wait_ge(kz_ready, l * 4 + 4)
                used(U_GATE)
                project(MIX0 + U_GATE, bank[0:24, 6, 0:SEQ], width=24)
                pe.wait_ge(v_ready, l * 2 + 2)
                for i in range(2):
                    pe.wait_ge(fl_ready, l * 2 + i + 1)
                    for b in range(4):
                        u = U_W1K + 4 * i + b
                        used(u)
                        s = (MIX0 + u) % RING
                        o = bank[0:N_KV * NC, 4 + i, 0:2 * P]
                        for k4 in range(4):
                            k = 4 * b + k4
                            wv = slice(k4 * 2 * P, (k4 + 1) * 2 * P)
                            mm(o, fh[:, i, k, :], whi[:, s, wv], start=(k == 0), stop=False)
                            mm(o, fl[:, i, k, :], whi[:, s, wv], start=False, stop=False)
                            m = mm(o, fh[:, i, k, :], wlo[:, s, wv], start=False, stop=(k == 15))
                        m.then_inc(unit_used, 1)
                        if i == 0 and b == 0:
                            pe.wait_ge(gT_ready, l + 1)
                            for t in range(QT):
                                m = mm(bank[:, 7, t * 24:(t + 1) * 24], gT[:, t * P:(t + 1) * P], ident[0:24, 0:24],
                                       start=True, stop=True, skip_group_check=True)
                            m.then_inc(gate_turned, 1)
                used(U_W2)
                pe.wait_ge(chid_ready, l * 2 + 2)
                for i in range(4):
                    nb = N_KV * NC
                    m = mm(bank[:, 6, i * nb:(i + 1) * nb], chid[:, i // 2, (i % 2) * P:(i % 2 + 1) * P], ident[0:nb, 0:nb],
                           start=True, stop=True, skip_group_check=True)
                m.then_inc(chid_turned, 1)
                last_unit2 = mm(bank[0:1, 5, 0:1], ones[:, 0:1], ones[:, 0:1], start=True, stop=True)
                last_unit2.then_inc(unit_used, 1)
                pe.wait_ge(chidT_ready, l + 1)
                pe.wait_ge(w2_ready, l + 1)
                pe.wait_ge(gate_ready, l + 1)
                nb = N_KV * NC
                for kt in range(2):
                    mm(bank[:, 7, 0:nb], w2[:, kt * P:(kt + 1) * P], chidT[:, kt * nb:(kt + 1) * nb],
                       start=(kt == 0), stop=(kt == 1), skip_group_check=True)
                for kv in range(N_KV):
                    for kt in range(2):
                        m = mm(bank[0:NC, 7, 64 + 64 * kv:128 + 64 * kv], chidT[:, (2 + kt) * nb + kv * NC:(2 + kt) * nb + (kv + 1) * NC],
                               w2[:, 256 + 64 * kt:320 + 64 * kt], start=(kt == 0), stop=(kt == 1), skip_group_check=True)
                m.then_inc(cmpkv_done, 1)
                pe.wait_ge(cmpkv_ready, l * 10 + 10)
                pe.wait_ge(q_ready, l * 4 + 4)
                for t in range(QT):
                    for c in range(GROUP):
                        a = (t * GROUP + c) * nb
                        m = mm(bank[:, 6, a:a + nb], qT[:, c, t * P:(t + 1) * P], kcz[:].rearrange("p a n -> p (a n)"),
                               start=True, stop=True, skip_group_check=True)
                m.then_inc(cscore_done, 1)

                def scores(n):
                    br, qt, segs = job(n)
                    if n >= 2:
                        pe.wait_ge(scored, l * N_JOBS + (n - 1))
                    if qt == 1:
                        m = mm(bank[:, 4 + n % 2, :], qT[:, segs[0][0], P:2 * P], kz[:, br].rearrange("p a t -> p (a t)"),
                               start=True, stop=True)
                    else:
                        for i in range(2):
                            m = mm(bank[:, 4 + n % 2, 2 * P * i:2 * P * (i + 1)], qT[:, segs[2 * i][0], 0:P], kz[:, br, :, 0:P],
                                   start=True, stop=True, skip_group_check=True)
                    m.then_inc(scores_done, 1)

                def turn(n):
                    pe.wait_ge(probs, l * N_JOBS + (n + 1))
                    if n >= 2:
                        pe.wait_ge(prT_ready, l * N_JOBS + (n - 1))
                    for i in range(4):
                        m = nc.tensor.transpose(bank[:, 6 + n % 2, i * P:(i + 1) * P], pr[:, n % 2, i * P:(i + 1) * P], ident[:])
                    m.then_inc(turned, 1)

                def values(n):
                    br, qt, segs = job(n)
                    pe.wait_ge(prT_ready, l * N_JOBS + (n + 1))
                    at = 0
                    for h, kb in segs:
                        kv = h // GROUP
                        for b in range(kb):
                            m = mm(bank[:, 2 * br + qt, h * HEAD_DIM:(h + 1) * HEAD_DIM], prT[:, n % 2, at:at + P],
                                   v[:, b, br * P + kv * 64:br * P + kv * 64 + 64],
                                   start=(b == 0 and segs[0][0] == 0 and h == 0), stop=(b == kb - 1), skip_group_check=True)
                            at += P
                    m.then_inc(pv_done, 1)

                scores(0)
                scores(1)
                pe.wait_ge(tap_done, l * TAPS + TAPS)
                for t in range(CT):
                    m = mm(bank[:, 2, 0:SEQ], ones[:], y[:, t, :], start=(t == 0), stop=(t == CT - 1))
                m.then_inc(ysum_ready, 1)
                pe.wait_ge(cs_step, l * 5 + 1)
                for n in range(N_JOBS):
                    turn(n)
                    if n + 2 < N_JOBS:
                        scores(n + 2)
                    if n == 6:
                        pe.wait_ge(ystd_ready, l + 1)
                    if n >= 1:
                        values(n - 1)
                    if n == 1:
                        pe.wait_ge(ysq_ready, l + 1)
                        for t in range(CT):
                            m = mm(bank[:, 3, 0:SEQ], ones[:], ysq[:, t, :], start=(t == 0), stop=(t == CT - 1))
                        m.then_inc(yvar_ready, 1)
                pe.wait_ge(cp_ready, l * 2 + 2)
                pe.wait_ge(prT_ready, l * N_JOBS + 11)
                for i in range(QT * N_KV):
                    m = nc.tensor.transpose(bank[:, 6, i * P:(i + 1) * P],
                                            cp[:, i // N_KV, i % N_KV].rearrange("p c n -> p (c n)"), ident[:])
                m.then_inc(cp_turned, 1)
                values(N_JOBS - 1)
                pe.wait_ge(cpT_ready, l + 1)
                for i in range(QT * N_KV):
                    t, kv = divmod(i, N_KV)
                    m = mm(bank[:, 4 + t, kv * 256:(kv + 1) * 256], cpT[:, t, kv, :], vcd[:, kv, :], start=True, stop=True,
                           skip_group_check=True)
                m.then_inc(cpv_done, 1)
                pe.wait_ge(o_step, l * 8 + 4)
                pe.wait_ge(cl_ready, l + 1)
                for t in range(CT):
                    used(U_OUT + t)
                    to_residual(MIX0 + U_OUT + t, ch[:, t, :], cl[:, t, :], t == 0, False).then_inc(unit_used, 1)
                pe.wait_ge(o_step, l * 8 + 8)
                for t in range(4):
                    for qt in range(QT):
                        m = nc.tensor.transpose(bank[:, 6 + t // 2, (t % 2) * SEQ + qt * P:(t % 2) * SEQ + (qt + 1) * P],
                                                oacc[:, qt, t * P:(t + 1) * P], ident[:])
                m.then_inc(o_turned, 1)
                for t in range(4):
                    used(U_OUT + 4 + t)
                    pe.wait_ge(al_ready, l * 2 + t // 2 + 1)
                    m = to_residual(MIX0 + U_OUT + 4 + t, ah[:, t, :], al[:, t, :], False, t == 3)
                    if t < 3:
                        m.then_inc(unit_used, 1)
                last_unit()
                sum_squares(l * 3 + 2, l * 12 + 8)
                ffn(l, 1, l * 24 + 16)
            sum_squares(DEPTH * 3, DEPTH * 12)


def _columns(wt, cols):
    import numpy as np
    a = wt[:, cols].reshape(-1, 128, len(cols)).transpose(1, 0, 2).reshape(128, -1)
    u = np.zeros((128, 1024), np.float32)
    u[:, :a.shape[1]] = a
    return u


def _stream(a):
    import numpy as np
    units = []
    for l in range(2):
        def ffn(g, u, d):
            g, u, d = a[g][l], a[u][l], a[d][l]
            def gu(c):
                cols = np.arange(c * 128, (c + 1) * 128)
                units.append(_columns(g, cols))
                units.append(_columns(u, cols))
            gu(0)
            for c in range(1, 22):
                gu(c)
                units.append(d[(c - 1) * 128:c * 128])
            units.append(d[21 * 128:])
        ffn("ffn1_w_gate", "ffn1_w_up", "ffn1_w_down")
        w = a["w_in"][l]
        q0, kc, vc, ks, vs, kw, vw, gl, ga, gb = np.cumsum([0, 512, 128, 128, 128, 128, 128, 128, 24, 512])
        r = np.arange
        for t in range(4):
            units.append(_columns(w, gb + t * 128 + r(128)))
            units.append(_columns(w, ga + t * 128 + r(128)))
        for o in (kc, vc, ks, kw):
            units.append(_columns(w, o + r(128)))
        for c in range(4):
            units.append(_columns(w, np.concatenate([q0 + c * 64 + r(64), q0 + (c + 4) * 64 + r(64)])))
        vv = np.concatenate([vs + r(128), vw + r(128)])
        units.append(_columns(w[:512], vv))
        units.append(_columns(w[512:], vv))
        units.append(_columns(w, gl + np.array([h * 3 + b for b in range(3) for h in range(8)])))
        for n in ("cmp_k_w1", "cmp_v_w1"):
            for b in range(4):
                units.append(_columns(a[n][l][b * 512:(b + 1) * 512], r(256)))
        u = np.zeros((128, 1024), np.float32)
        for kt in range(2):
            k2 = a["cmp_k_w2"][l][kt * 128:(kt + 1) * 128]
            u[:, kt * 128:kt * 128 + 64] = k2
            u[:, kt * 128 + 64:kt * 128 + 128] = k2
            u[:, 256 + kt * 64:320 + kt * 64] = a["cmp_v_w2"][l][kt * 128:(kt + 1) * 128]
        units.append(u)
        for t in (4, 5, 6, 7, 0, 1, 2, 3):
            units.append(a["w_out"][l][t * 128:(t + 1) * 128])
        ffn("ffn2_w_gate", "ffn2_w_up", "ffn2_w_down")
    return np.stack(units)


def _params(a):
    import numpy as np
    cols = []
    tile = lambda vec: vec.reshape(-1, 128)
    for l in range(2):
        for n in ("ffn1_norm", "mix_norm", "ffn2_norm", "conv_b", "conv_norm_g", "conv_norm_b"):
            cols.append(tile(a[n][l]))
        cols.append(tile(a["conv_w"][l]))
        cols.append(tile(a["cmp_pos_k"][l]))
        cols.append(tile(a["cmp_pos_v"][l]))
    cols.append(tile(a["final_norm"]))
    return np.ascontiguousarray(np.concatenate(cols).T)


def _tables():
    import numpy as np
    slope = 2.0 ** (-8.0 * np.arange(1, 9) / 8)
    q, k = np.arange(128)[:, None], np.arange(256)[None]
    d = 128 + q - k
    bias = np.where(d[:, None, :] >= 0, -8.0 * slope[None, :, None] * d[:, None, :], -1e31).astype(np.float32)
    t = (np.arange(2)[None, :, None] * 128 + np.arange(128)[:, None, None])
    end = (np.arange(15) * 16 + 31)[None, None, :]
    dc = t - end
    sl = slope.reshape(2, 4).T.reshape(8)
    full = np.broadcast_to(dc[:, :, None, :], (128, 2, 8, 15))
    cb = np.where(full >= 0, -sl[None, None, :, None] * full, -1e30).astype(np.float32).reshape(128, 240)
    ok = (full >= 0).astype(np.float32).reshape(128, 240)
    return np.ascontiguousarray(bias), np.ascontiguousarray(cb), np.ascontiguousarray(ok)


def kernel(**inputs):
    import numpy as np
    import concourse.bacc as bacc
    from concourse.bass_utils import run_bass_kernel_spmd

    a = {k: np.asarray(v) for k, v in inputs.items()}
    bias, cb, ok = _tables()
    xT = np.ascontiguousarray(a["x"][0].T.reshape(8, 128, 256).transpose(1, 0, 2))
    arrays = {"w": _stream(a), "xT": xT, "params": _params(a), "bias": bias, "cbias": cb, "cmask": ok,
              "eye": np.eye(128, dtype=np.float32)}
    nc = bacc.Bacc("TRN2", target_bir_lowering=False, num_devices=1)
    aps = [nc.dram_tensor(n, v.shape, F32, kind="ExternalInput").ap() for n, v in arrays.items()]
    out = nc.dram_tensor("outT", (128, 8, 256), F32, kind="ExternalOutput").ap()
    trunk(nc, *aps, out)
    r = run_bass_kernel_spmd(nc, [arrays], core_ids=[0])
    o = r.results[0]["outT"]
    return np.ascontiguousarray(o.transpose(1, 0, 2).reshape(1024, 256).T)[None]
```

```python
import concourse.bass as bass
from concourse import mybir

F32 = mybir.dt.float32
F32R = mybir.dt.float32r
ALU = mybir.AluOpType
ACT = mybir.ActivationFunctionType
AX = mybir.AxisListType

P = 128
D_MODEL, SEQ, DEPTH = 1024, 256, 2
N_HEADS, HEAD_DIM, N_KV = 8, 64, 2
GROUP = N_HEADS // N_KV
D_FF = 2816
CONV_CH, CONV_WIDTH = 512, 31
PAD = CONV_WIDTH - 1
CMP_BLOCK, CMP_STRIDE = 32, 16
NC = SEQ // CMP_STRIDE - 1
EPS = 1e-6
BIG = 3.0e38

KT = D_MODEL // P
QT = SEQ // P
CT = CONV_CH // P
FC = D_FF // P
BANK = 512
UNIT = 1024
RING = 6

FFN_UNITS = 3 * FC
U_GLU, U_KC, U_VC, U_KS, U_KW, U_Q, U_V, U_GATE, U_W1K, U_W1V, U_W2, U_OUT = 0, 8, 9, 10, 11, 12, 16, 18, 19, 23, 27, 28
MIX_UNITS = 36
MIX0 = FFN_UNITS
FFN2_0 = MIX0 + MIX_UNITS
LAYER_UNITS = FFN2_0 + FFN_UNITS
assert MIX0 % RING == 0 and FFN2_0 % RING == 0 and LAYER_UNITS % RING == 0

C_N1, C_NM, C_N2 = 0, KT, 2 * KT
C_CB = 3 * KT
C_CG = C_CB + CT
C_CBETA = C_CG + CT
C_CW = C_CBETA + CT
C_POS = C_CW + CONV_WIDTH * CT
LAYER_COLS = C_POS + 2 * (CMP_BLOCK // 2)

N_JOBS = 12
TAPS = CONV_WIDTH * CT
TAP_TILES = [(2, (3, [0])), (4, (8, [0, 1])), (6, (12, [0, 1, 2]))]
TAPS_PROJ = [1, 2, 3, 3, 3, 3] + [4] * 11
TAPS_JOB = [5] * 8 + [6] * 4


def unit_g(c):
    return 0 if c == 0 else 2 + 3 * (c - 1)


def unit_d(c):
    return FFN_UNITS - 1 if c == FC - 1 else unit_g(c + 1) + 2


def job(n):
    br, m = divmod(n, 6)
    if m < 4:
        return br, 1, [(m, 2), (m + GROUP, 2)]
    g = 2 * (m - 4)
    return br, 0, [(g, 1), (g + GROUP, 1), (g + 1, 1), (g + 1 + GROUP, 1)]


def trunk(nc, w, xT, params, bias, cbias, cmask, eye, out):
    from contextlib import ExitStack
    ctx = ExitStack()
    with ctx:
        sb = lambda name, shape, dt=F32: ctx.enter_context(nc.sbuf_tensor(name, shape, dt))
        sem = lambda name: ctx.enter_context(nc.semaphore(name))
        bank = ctx.enter_context(nc.psum_tensor("bank", [P, 8, BANK], F32))

        raw = sb("raw", [P, RING, UNIT])
        whi = sb("whi", [P, RING, UNIT], F32R)
        wlo = sb("wlo", [P, RING, UNIT], F32R)
        x = sb("x", [P, KT, SEQ])
        sq = sb("sq", [P, KT, SEQ])
        xn = sb("xn", [P, KT, SEQ])
        xh = sb("xh", [P, KT, SEQ], F32R)
        xl = sb("xl", [P, KT, SEQ], F32R)
        std = sb("std", [P, SEQ])
        rstd = sb("rstd", [P, SEQ])
        sil = sb("sil", [P, 2, SEQ])
        up = sb("up", [P, 2, SEQ])
        hid = sb("hid", [P, 2, SEQ])
        hh = sb("hh", [P, 2, SEQ], F32R)
        hl = sb("hl", [P, 2, SEQ], F32R)
        table = sb("table", [P, DEPTH * LAYER_COLS + KT])
        cur = sb("cur", [P, LAYER_COLS])
        alibi = sb("alibi", [P, N_HEADS, 2 * P])
        calibi = sb("calibi", [P, QT * N_HEADS * NC])
        cok = sb("cok", [P, QT * N_HEADS * NC])
        ident = sb("ident", [P, P])
        ones = sb("ones", [P, P])
        eps = sb("eps", [P, 1])
        sig = sb("sig", [P, 2, SEQ])
        upad = sb("upad", [P, CT, PAD + SEQ])
        y = sb("y", [P, CT, SEQ])
        mu = sb("mu", [P, SEQ])
        yc = sb("yc", [P, CT, SEQ])
        ysq = sb("ysq", [P, CT, SEQ])
        ystd = sb("ystd", [P, SEQ])
        yrstd = sb("yrstd", [P, SEQ])
        yn, cz = ysq, yc
        qT = sb("qT", [P, GROUP, SEQ])
        kz = sb("kz", [P, 2, N_KV, SEQ])
        v = sb("v", [P, QT, 2 * P])
        gT = sb("gT", [24, SEQ])
        gate = sb("gate", [P, QT, 24])
        kk = sb("kk", [P, 2, N_KV, SEQ])
        flat = sb("flat", [P, 2, CMP_BLOCK // 2, N_KV * NC])
        fh = sb("fh", [P, 2, CMP_BLOCK // 2, N_KV * NC], F32R)
        fl = sb("fl", [P, 2, CMP_BLOCK // 2, N_KV * NC], F32R)
        w2 = sb("w2", [P, 384])
        chid = sb("chid", [N_KV * NC, 2, 2 * P])
        chidT = sb("chidT", [P, 4 * N_KV * NC])
        kcz = sb("kcz", [P, N_KV, NC])
        vcd = sb("vcd", [P, N_KV, GROUP * HEAD_DIM])
        cs = sb("cs", [P, QT * N_HEADS, NC])
        cmx = sb("cmx", [P, QT * N_HEADS])
        ce = sb("ce", [P, QT * N_HEADS, NC])
        csum = sb("csum", [P, QT * N_HEADS])
        cp = sb("cp", [P, QT, N_KV, GROUP, 32])
        cpT = sb("cpT", [P, QT, N_KV, P])
        ah, ch = xh[:, 0:4, :], xh[:, 4:KT, :]
        al, cl = xl[:, 0:4, :], xl[:, 4:KT, :]
        pr = xn[:, 0:4, :].rearrange("p (b a) t -> p b (a t)", b=2)
        held = sb("held", [P, 2])
        nmax = sb("nmax", [P, 2, 4])
        prT = xn[:, 4:8, :].rearrange("p (b a) t -> p b (a t)", b=2)
        rsum = sb("rsum", [P, 2, QT, N_HEADS])
        rrec = sb("rrec", [P, 3, QT, N_HEADS])
        fac = sb("fac", [P, 3, QT, N_HEADS])
        oacc = sb("oacc", [P, QT, BANK])
        otmp = sq[:].rearrange("p (b t a) s -> p b t (a s)", b=2, t=QT)

        landed = [sem(f"landed{s}") for s in range(RING)]
        x_in = [sem(f"x_in{b}") for b in range(4)]
        table_in, consts_in, out_done = sem("table_in"), sem("consts_in"), sem("out_done")
        setup_done = sem("setup_done")
        cur_ready = sem("cur_ready")
        hi_ready, lo_ready, unit_used = sem("hi_ready"), sem("lo_ready"), sem("unit_used")
        x_ready, sq_ready, ssum_ready = sem("x_ready"), sem("sq_ready"), sem("ssum_ready")
        std_ready, rstd_ready = sem("std_ready"), sem("rstd_ready")
        xn_ready, xh_ready, xl_ready = sem("xn_ready"), sem("xh_ready"), sem("xl_ready")
        y_ready = sem("y_ready")
        gn_ready, un_ready = sem("gn_ready"), sem("un_ready")
        sil_ready, hid_ready, hh_ready, hl_ready = sem("sil_ready"), sem("hid_ready"), sem("hh_ready"), sem("hl_ready")
        sig_ready, glu_ready, tap_done = sem("sig_ready"), sem("glu_ready"), sem("tap_done")
        ysum_ready, mu_ready, yc_ready, ysq_ready = sem("ysum_ready"), sem("mu_ready"), sem("yc_ready"), sem("ysq_ready")
        yvar_ready, ystd_ready, yrstd_ready, yn_ready = sem("yvar_ready"), sem("ystd_ready"), sem("yrstd_ready"), sem("yn_ready")
        cz_ready, ch_ready, cl_ready = sem("cz_ready"), sem("ch_ready"), sem("cl_ready")
        kk_ready, kz_ready, q_ready, v_ready = sem("kk_ready"), sem("kz_ready"), sem("q_ready"), sem("v_ready")
        gT_ready, gate_turned, gate_ready = sem("gT_ready"), sem("gate_turned"), sem("gate_ready")
        flat_ready, fh_ready, fl_ready = sem("flat_ready"), sem("fh_ready"), sem("fl_ready")
        w2_ready, chid_ready, chid_turned, chidT_ready = sem("w2_ready"), sem("chid_ready"), sem("chid_turned"), sem("chidT_ready")
        cmpkv_done, cmpkv_ready, cscore_done = sem("cmpkv_done"), sem("cmpkv_ready"), sem("cscore_done")
        cs_step, ce_ready, cp_ready, cp_turned, cpT_ready, cpv_done = (
            sem("cs_step"), sem("ce_ready"), sem("cp_ready"), sem("cp_turned"), sem("cpT_ready"), sem("cpv_done"))
        scores_done, scored, probs, turned, prT_ready, pv_done = (
            sem("scores_done"), sem("scored"), sem("probs"), sem("turned"), sem("prT_ready"), sem("pv_done"))
        fac_step, o_step, o_turned, ah_ready, al_ready = (
            sem("fac_step"), sem("o_step"), sem("o_turned"), sem("ah_ready"), sem("al_ready"))

        block = ctx.enter_context(nc.Block())
        f32 = lambda ap: ap.bitcast(F32)

        @block.sync
        def _(sp):
            for b in range(4):
                sp.dma_start(xn[:, 2 * b:2 * b + 2, :], xT[:, 2 * b:2 * b + 2, :]).then_inc(x_in[b], 16)
                if b == 0:
                    sp.dma_start(table[:], params).then_inc(table_in, 16)
                    sp.dma_start(raw[:, 0, :], w[0]).then_inc(landed[0], 16)
            for s in range(1, RING):
                sp.dma_start(raw[:, s, :], w[s]).then_inc(landed[s], 16)
            sp.dma_start(ident[:], eye).then_inc(consts_in, 16)
            sp.dma_start(alibi[:], bias).then_inc(consts_in, 16)
            sp.dma_start(calibi[:], cbias).then_inc(consts_in, 16)
            sp.dma_start(cok[:], cmask).then_inc(consts_in, 16)
            with sp.Fori(1, DEPTH * LAYER_UNITS // RING) as r:
                for s in range(RING):
                    sp.wait_ge(lo_ready, r * RING + (s - RING + 1))
                    sp.dma_start(raw[:, s, :], w[r * RING + s]).then_inc(landed[s], 16)
            for k in range(KT):
                sp.wait_ge(xn_ready, DEPTH * KT + k + 1)
                sp.dma_start(out[:, k, :], xn[:, k, :]).then_inc(out_done, 16)
            sp.wait_ge(out_done, 16 * KT)

        @block.gpsimd
        def _(pool):
            nc.gpsimd.memset(upad[:, :, 0:PAD], 0.0).then_inc(setup_done, 1)
            nc.gpsimd.memset(kz[:], 0.0).then_inc(setup_done, 1)
            nc.gpsimd.memset(kcz[:], 0.0).then_inc(setup_done, 1)
            nc.gpsimd.memset(vcd[:], 0.0).then_inc(setup_done, 1)
            nc.gpsimd.memset(cp[:], 0.0).then_inc(setup_done, 1)
            nc.gpsimd.memset(ones[:], 1.0).then_inc(setup_done, 1)
            nc.gpsimd.memset(eps[:], EPS).then_inc(setup_done, 1)

        SETUP = 7

        @block.scalar
        def _(act):
            def hi(l, n):
                act.wait_ge(landed[n % RING], l * (16 * LAYER_UNITS // RING) + 16 * (n // RING + 1))
                if n >= RING:
                    act.wait_ge(unit_used, l * LAYER_UNITS + (n - RING + 1))
                nc.scalar.copy(whi[:, n % RING, :], raw[:, n % RING, :]).then_inc(hi_ready, 1)

            def hi_in_loop(l, j, n):
                act.wait_ge(landed[n % RING], l * (16 * LAYER_UNITS // RING) + j * 16 + 16 * (n // RING + 1))
                act.wait_ge(unit_used, l * LAYER_UNITS + j * RING + (n - RING + 1))
                nc.scalar.copy(whi[:, n % RING, :], raw[:, n % RING, :]).then_inc(hi_ready, 1)

            def square(q4, b):
                act.wait_ge(x_ready, q4 + (b + 1))
                nc.scalar.activation(sq[:, 2 * b:2 * b + 2, :], x[:, 2 * b:2 * b + 2, :], ACT.Square).then_inc(sq_ready, 1)

            def root(q, src):
                act.wait_ge(ssum_ready, q + 1)
                nc.scalar.activation(std[:], src, ACT.Sqrt, scale=1.0 / D_MODEL, bias=eps[:, 0:1]).then_inc(std_ready, 1)

            def scaled_high(l, q4, x8, gains):
                act.wait_ge(cur_ready, l + 1)
                for k in range(KT):
                    if k % 2 == 0:
                        act.wait_ge(x_ready, q4 + (k // 2 + 1))
                    nc.scalar.mul(xh[:, k, :], x[:, k, :], gains[:, k:k + 1]).then_inc(xh_ready, 1)

            def high_x(x8, n8):
                for k in range(KT):
                    act.wait_ge(xn_ready, n8 + (k + 1))
                    nc.scalar.copy(xh[:, k, :], xn[:, k, :]).then_inc(xh_ready, 1)

            def silu(l, f, j, c):
                act.wait_ge(gn_ready, l * 2 * FC + j * 2 + (f * FC + c + 1))
                nc.scalar.activation(sil[:, c % 2, :], sil[:, c % 2, :], ACT.Silu).then_inc(sil_ready, 1)

            def ffn(l, f):
                base = FFN2_0 if f else 0

                def steps(c, j=None):
                    for i, n in enumerate(range(unit_g(c), min(unit_g(c + 1), FFN_UNITS - 1))):
                        if base + n + RING < LAYER_UNITS:
                            if j is None:
                                hi(l, base + n + RING)
                            else:
                                hi_in_loop(l, j, base + n + RING)
                        if i == 0:
                            silu(l, f, 0 if j is None else j, c)

                steps(0)
                steps(1)
                with act.Fori(0, (FC - 4) // 2) as j:
                    steps(2, j)
                    steps(3, j)
                steps(FC - 2)
                steps(FC - 1)

            act.wait_ge(setup_done, SETUP)
            with act.Fori(0, DEPTH) as l:
                hi(l, 0)
                scaled_high(l, l * 12, l * 24, cur[:, C_N1:C_N1 + KT])
                hi(l, 1)
                for b in range(4):
                    square(l * 12, b)
                root(l * 3, bank[:, 0, 0:SEQ])
                for n in range(2, RING):
                    hi(l, n)
                ffn(l, 0)

                for b in range(4):
                    square(l * 12 + 4, b)
                hi(l, MIX0 - 1 + RING)
                root(l * 3 + 1, bank[:, 7, 0:SEQ])
                high_x(l * 24 + 8, l * 8)

                def done(u):
                    act.wait_ge(unit_used, l * LAYER_UNITS + (MIX0 + u + 1))

                def exps(n):
                    br, qt, segs = job(n)
                    act.wait_ge(scored, l * N_JOBS + (n + 1))
                    at = 0
                    for i, (h, kb) in enumerate(segs):
                        p = pr[:, n % 2, at:at + P * kb]
                        e = nc.scalar.activation(p, p, ACT.Exp, scale=-1.0, bias=nmax[:, n % 2, i:i + 1],
                                                 accum_out=rsum[:, br, qt, h:h + 1])
                        at += P * kb
                    e.then_inc(probs, 1)

                def copy_prT(n):
                    act.wait_ge(turned, l * N_JOBS + (n + 1))
                    if n >= 2:
                        act.wait_ge(pv_done, l * N_JOBS + (n - 1))
                    nc.scalar.copy(prT[:, n % 2, :], bank[:, 6, :]).then_inc(prT_ready, 1)

                for u in range(U_W1K):
                    done(u)
                    if u < U_KC and u % 2 == 0:
                        t = u // 2 % 2
                        nc.scalar.activation(sig[:, t, :], bank[:, 4 + 2 * t, 0:SEQ], ACT.Sigmoid).then_inc(sig_ready, 1)
                    if u in (U_KC, U_VC):
                        i = u - U_KC
                        for kv in range(N_KV):
                            src = bank[64 * kv:64 * kv + 64, 4 + i, :]
                            nc.scalar.copy(kk[0:64, i, kv, :], src[:, 0:SEQ]).then_inc(kk_ready, 1)
                            nc.scalar.copy(kk[64:128, i, kv, 0:SEQ - 1], src[:, 1:SEQ]).then_inc(kk_ready, 1)
                    if u in (U_KS, U_KW):
                        i = u - U_KS
                        for kv in range(N_KV):
                            r = slice(64 * kv, 64 * kv + 64)
                            nc.scalar.copy(kz[r, i, kv, :], bank[r, 6 + i, 0:SEQ]).then_inc(kz_ready, 1)
                    if U_Q <= u < U_V:
                        nc.scalar.copy(qT[:, u - U_Q, :], bank[:, u - U_Q, 0:SEQ]).then_inc(q_ready, 1)
                        if u < U_Q + 2:
                            i = u - U_Q
                            act.wait_ge(flat_ready, l * 8 + 4 * i + 4)
                            nc.scalar.copy(fh[:, i], flat[:, i]).then_inc(fh_ready, 1)
                    if u == U_V + 1:
                        for t in range(QT):
                            nc.scalar.copy(v[:, t, :], bank[:, 4 + t, 0:SEQ]).then_inc(v_ready, 1)
                    if u == U_GATE:
                        nc.scalar.activation(gT[:], bank[0:24, 6, 0:SEQ], ACT.Sigmoid).then_inc(gT_ready, 1)
                    hi(l, MIX0 + u + RING)
                exps(0)
                exps(1)
                for n in range(N_JOBS):
                    copy_prT(n)
                    if n + 2 < N_JOBS:
                        exps(n + 2)
                    if n < 8:
                        if n % 4 == 3:
                            i = n // 4
                            done(U_W1K + n)
                            nc.scalar.activation(chid[:, i, :], bank[0:N_KV * NC, 7, 0:2 * P], ACT.Silu).then_inc(chid_ready, 1)
                        hi(l, MIX0 + U_W1K + n + RING)
                    if n == 8:
                        act.wait_ge(chid_turned, l + 1)
                        nc.scalar.copy(chidT[:], bank[:, 7, 0:4 * N_KV * NC]).then_inc(chidT_ready, 1)
                        nc.scalar.copy(gate[:], bank[:, 7, 128:128 + QT * 24].rearrange("p (t g) -> p t g", t=QT)).then_inc(gate_ready, 1)
                        hi(l, MIX0 + U_W2 + RING)
                    if n == 9:
                        act.wait_ge(cmpkv_done, l + 1)
                        for kv in range(N_KV):
                            r = slice(64 * kv, 64 * kv + 64)
                            nc.scalar.copy(kcz[r, kv, :], bank[r, 7, kv * NC:(kv + 1) * NC]).then_inc(cmpkv_ready, 1)
                        for kv in range(N_KV):
                            for g in range(GROUP):
                                nc.scalar.copy(vcd[32 * g:32 * g + NC, kv, g * HEAD_DIM:(g + 1) * HEAD_DIM],
                                               bank[0:NC, 7, 64 + 64 * kv:128 + 64 * kv]).then_inc(cmpkv_ready, 1)
                act.wait_ge(cs_step, l * 5 + 3)
                nc.scalar.activation(ce[:], cs[:], ACT.Exp).then_inc(ce_ready, 1)
                act.wait_ge(yc_ready, l + 1)
                nc.scalar.activation(ysq[:], yc[:], ACT.Square).then_inc(ysq_ready, 1)
                act.wait_ge(cp_turned, l + 1)
                nc.scalar.copy(cpT[:].rearrange("p t k q -> p (t k q)"), bank[:, 6, :]).then_inc(cpT_ready, 1)
                act.wait_ge(yvar_ready, l + 1)
                nc.scalar.activation(ystd[:], bank[:, 1, 0:SEQ], ACT.Sqrt, scale=1.0 / CONV_CH,
                                     bias=eps[:, 0:1]).then_inc(ystd_ready, 1)
                act.wait_ge(o_turned, l + 1)
                for b in range(2):
                    nc.scalar.copy(ah[:, 2 * b:2 * b + 2, :], bank[:, 6 + b, :]).then_inc(ah_ready, 1)
                act.wait_ge(yn_ready, l + 1)
                for t in range(CT):
                    nc.scalar.activation(cz[:, t, :], yn[:, t, :], ACT.Silu, scale=cur[:, C_CG + t:C_CG + t + 1],
                                         bias=cur[:, C_CBETA + t:C_CBETA + t + 1]).then_inc(cz_ready, 1)
                for t in range(CT):
                    act.wait_ge(cz_ready, l * CT + (t + 1))
                    nc.scalar.copy(ch[:, t, :], cz[:, t, :]).then_inc(ch_ready, 1)
                for u in range(U_OUT, MIX_UNITS - 1):
                    hi(l, MIX0 + u + RING)

                scaled_high(l, l * 12 + 8, l * 24 + 16, cur[:, C_N2:C_N2 + KT])
                hi(l, FFN2_0 - 1 + RING)
                for b in range(4):
                    square(l * 12 + 8, b)
                root(l * 3 + 2, bank[:, 0, 0:SEQ])
                ffn(l, 1)
            for b in range(4):
                square(DEPTH * 12, b)
            root(DEPTH * 3, bank[:, 7, 0:SEQ])

        @block.vector
        def _(dve):
            def lo(l, n):
                dve.wait_ge(hi_ready, l * LAYER_UNITS + (n + 1))
                nc.vector.tensor_tensor(wlo[:, n % RING, :], raw[:, n % RING, :], f32(whi[:, n % RING, :]),
                                        ALU.subtract).then_inc(lo_ready, 1)

            def lo_in_loop(l, j, n):
                dve.wait_ge(hi_ready, l * LAYER_UNITS + j * RING + (n + 1))
                nc.vector.tensor_tensor(wlo[:, n % RING, :], raw[:, n % RING, :], f32(whi[:, n % RING, :]),
                                        ALU.subtract).then_inc(lo_ready, 1)

            def residual(y4, scale):
                for b in range(4):
                    dve.wait_ge(y_ready, y4 + (b + 1))
                    xb = x[:, 2 * b:2 * b + 2, :].rearrange("p a t -> p (a t)")
                    nc.vector.scalar_tensor_tensor(out=xb, in0=bank[:, b, :], scalar=scale, in1=xb,
                                                   op0=ALU.mult, op1=ALU.add).then_inc(x_ready, 1)

            def recip(q):
                dve.wait_ge(std_ready, q + 1)
                nc.vector.reciprocal(rstd[:], std[:]).then_inc(rstd_ready, 1)
                dve.wait_ge(rstd_ready, q + 1)

            def normed(k, gains):
                nc.vector.scalar_tensor_tensor(out=xn[:, k, :], in0=x[:, k, :], scalar=gains[:, k:k + 1],
                                               in1=rstd[:], op0=ALU.mult, op1=ALU.mult).then_inc(xn_ready, 1)

            def low_x(x8, k):
                dve.wait_ge(xh_ready, x8 + (k + 1))
                nc.vector.tensor_tensor(xl[:, k, :], xn[:, k, :], f32(xh[:, k, :]), ALU.subtract).then_inc(xl_ready, 1)

            def scaled_low(x8, gains):
                for k in range(KT):
                    dve.wait_ge(xh_ready, x8 + (k + 1))
                    nc.vector.scalar_tensor_tensor(out=xl[:, k, :], in0=x[:, k, :], scalar=gains[:, k:k + 1],
                                                   in1=f32(xh[:, k, :]), op0=ALU.mult, op1=ALU.subtract).then_inc(xl_ready, 1)

            def gate_normed(l, f, j, c):
                dve.wait_ge(unit_used, l * LAYER_UNITS + j * RING + ((FFN2_0 if f else 0) + unit_g(c) + 1))
                b = c % 2
                nc.vector.tensor_tensor(sil[:, b, :], bank[:, 4 + 2 * b, 0:SEQ], rstd[:], ALU.mult).then_inc(gn_ready, 1)

            def hidden(l, f, j, c):
                h0 = f * FC + c + 1
                b = c % 2
                dve.wait_ge(unit_used, l * LAYER_UNITS + j * RING + ((FFN2_0 if f else 0) + unit_g(c) + 2))
                nc.vector.tensor_tensor(up[:, b, :], bank[:, 5 + 2 * b, 0:SEQ], rstd[:], ALU.mult).then_inc(un_ready, 1)
                dve.wait_ge(un_ready, l * 2 * FC + j * 2 + h0)
                dve.wait_ge(sil_ready, l * 2 * FC + j * 2 + h0)
                nc.vector.tensor_tensor(hid[:, b, :], up[:, b, :], sil[:, b, :], ALU.mult).then_inc(hid_ready, 1)
                dve.wait_ge(hid_ready, l * 2 * FC + j * 2 + h0)
                nc.vector.tensor_copy(hh[:, b, :], hid[:, b, :]).then_inc(hh_ready, 1)
                dve.wait_ge(hh_ready, l * 2 * FC + j * 2 + h0)
                nc.vector.tensor_tensor(hl[:, b, :], hid[:, b, :], f32(hh[:, b, :]), ALU.subtract).then_inc(hl_ready, 1)

            def ffn(l, f):
                base = FFN2_0 if f else 0

                def steps(c, j=None):
                    for i, n in enumerate(range(unit_g(c), min(unit_g(c + 1), FFN_UNITS - 1))):
                        if i == 0:
                            gate_normed(l, f, 0 if j is None else j, c)
                        if i == 1:
                            hidden(l, f, 0 if j is None else j, c)
                        if base + n + RING < LAYER_UNITS:
                            if j is None:
                                lo(l, base + n + RING)
                            else:
                                lo_in_loop(l, j, base + n + RING)

                steps(0)
                steps(1)
                with dve.Fori(0, (FC - 4) // 2) as j:
                    steps(2, j)
                    steps(3, j)
                steps(FC - 2)
                steps(FC - 1)

            dve.wait_ge(setup_done, SETUP)
            for b in range(4):
                dve.wait_ge(x_in[b], 16)
                nc.vector.tensor_copy(x[:, 2 * b:2 * b + 2, :], xn[:, 2 * b:2 * b + 2, :]).then_inc(x_ready, 1)
            dve.wait_ge(table_in, 16)
            with dve.Fori(0, DEPTH) as l:
                nc.vector.tensor_copy(cur[:], table[:, bass.ds(l * LAYER_COLS, LAYER_COLS)]).then_inc(cur_ready, 1)
                lo(l, 0)
                dve.wait_ge(cur_ready, l + 1)
                scaled_low(l * 24, cur[:, C_N1:C_N1 + KT])
                lo(l, 1)
                recip(l * 3)
                for n in range(2, RING):
                    lo(l, n)
                ffn(l, 0)
                residual(l * 12, 0.5)

                lo(l, MIX0 - 1 + RING)
                recip(l * 3 + 1)
                for k in range(KT + 1):
                    if k < KT:
                        normed(k, cur[:, C_NM:C_NM + KT])
                    if k:
                        low_x(l * 24 + 8, k - 1)

                def done(u):
                    dve.wait_ge(unit_used, l * LAYER_UNITS + (MIX0 + u + 1))

                tap_order, left = [], [list(range(CONV_WIDTH)) for _ in range(CT)]
                for _, (count, tiles) in TAP_TILES:
                    for i in range(count):
                        t = tiles[i % len(tiles)]
                        if left[t]:
                            tap_order.append((left[t].pop(0), t))
                while any(left):
                    for t in range(CT):
                        if left[t]:
                            tap_order.append((left[t].pop(0), t))
                place = {jt: i for i, jt in enumerate(tap_order)}
                next_tap = [0]

                def taps(n):
                    for i in range(next_tap[0], min(next_tap[0] + n, TAPS)):
                        j, t = tap_order[i]
                        wj = cur[:, C_CW + j * CT + t:C_CW + j * CT + t + 1]
                        src = upad[:, t, j:j + SEQ]
                        if j == 0:
                            dve.wait_ge(glu_ready, l * CT + (t + 1))
                            nc.vector.tensor_scalar(y[:, t, :], src, wj, cur[:, C_CB + t:C_CB + t + 1],
                                                    ALU.mult, ALU.add).then_inc(tap_done, 1)
                        else:
                            dve.wait_ge(tap_done, l * TAPS + (place[j - 1, t] + 1))
                            nc.vector.scalar_tensor_tensor(out=y[:, t, :], in0=src, scalar=wj, in1=y[:, t, :],
                                                           op0=ALU.mult, op1=ALU.add).then_inc(tap_done, 1)
                    next_tap[0] = min(next_tap[0] + n, TAPS)

                def score(n):
                    br, qt, segs = job(n)
                    dve.wait_ge(scores_done, l * N_JOBS + (n + 1))
                    if n >= 2:
                        dve.wait_ge(turned, l * N_JOBS + (n - 1))
                    nc.vector.memset(held[:, n % 2:n % 2 + 1], 0.0)
                    at = 0
                    for i, (h, kb) in enumerate(segs):
                        s = nc.vector.tensor_tensor_reduce(
                            pr[:, n % 2, at:at + P * kb], bank[:, 4 + n % 2, at:at + P * kb], alibi[:, h, 2 * P - P * kb:],
                            -(HEAD_DIM ** -0.5), BIG, ALU.add, ALU.min, nmax[:, n % 2, i:i + 1])
                        at += P * kb
                    s.then_inc(scored, 1)

                def factors(b, sums, gates, k0):
                    nc.vector.reciprocal(rrec[:, b], sums).then_inc(fac_step, 1)
                    dve.wait_ge(fac_step, l * 6 + k0 + 1)
                    nc.vector.tensor_tensor(fac[:, b], rrec[:, b], gates, ALU.mult).then_inc(fac_step, 1)
                    dve.wait_ge(fac_step, l * 6 + k0 + 2)

                def weigh(dst, src, b, qt):
                    nc.vector.tensor_tensor(
                        dst.rearrange("p (h d) -> p h d", h=N_HEADS), src.rearrange("p (h d) -> p h d", h=N_HEADS),
                        fac[:, b, qt, :].rearrange("p (h o) -> p h o", o=1).to_broadcast([P, N_HEADS, HEAD_DIM]),
                        ALU.mult).then_inc(o_step, 1)

                for u in range(U_W1K):
                    if u in (U_VC + 1, U_VC + 2):
                        i = u - U_VC - 1
                        dve.wait_ge(kk_ready, l * 8 + 4 * i + 4)
                        for kv in range(N_KV):
                            src = kk[:, i, kv, :].rearrange("p (n s) -> p s n", s=CMP_STRIDE)
                            for half in range(2):
                                a = src[:, 0:CMP_STRIDE:2, half:half + NC]
                                pos = cur[:, C_POS + 16 * i + 8 * half:C_POS + 16 * i + 8 * half + 8]
                                nc.vector.tensor_tensor(
                                    flat[:, i, 8 * half:8 * half + 8, kv * NC:(kv + 1) * NC], a,
                                    pos.rearrange("p (j o) -> p j o", o=1).to_broadcast([P, 8, NC]), ALU.add).then_inc(flat_ready, 1)
                    if u >= 2:
                        taps(TAPS_PROJ[u - 2])
                    if u < U_KC and u % 2 == 1:
                        t = u // 2
                        done(u)
                        dve.wait_ge(sig_ready, l * CT + (t + 1))
                        nc.vector.tensor_tensor(upad[:, t, PAD:PAD + SEQ], bank[:, 5 + 2 * (t % 2), 0:SEQ],
                                                sig[:, t % 2, :], ALU.mult).then_inc(glu_ready, 1)
                    if u in (U_Q + 2, U_Q + 3):
                        i = u - U_Q - 2
                        dve.wait_ge(fh_ready, l * 2 + i + 1)
                        nc.vector.tensor_tensor(fl[:, i], flat[:, i], f32(fh[:, i]), ALU.subtract).then_inc(fl_ready, 1)
                    lo(l, MIX0 + u + RING)
                dve.wait_ge(consts_in, 16 * 4)
                score(0)
                score(1)
                for n in range(N_JOBS):
                    if n + 2 < N_JOBS:
                        score(n + 2)
                    taps(TAPS_JOB[n])
                    if U_W1K + n + RING == U_W2:
                        dve.wait_ge(landed[(MIX0 + U_W2) % RING], l * (16 * LAYER_UNITS // RING) + 16 * ((MIX0 + U_W2) // RING + 1))
                        nc.vector.tensor_copy(w2[:], raw[:, (MIX0 + U_W2) % RING, 0:384]).then_inc(w2_ready, 1)
                    if n < 9:
                        lo(l, MIX0 + U_W1K + n + RING)
                    if n == 9:
                        gsel = gate[:].rearrange("p t (b h) -> p t b h", b=3)
                        dve.wait_ge(gate_ready, l + 1)
                        dve.wait_ge(probs, l * N_JOBS + 6)
                        factors(1, rsum[:, 0], gsel[:, :, 1, :], 0)
                        dve.wait_ge(pv_done, l * N_JOBS + 6)
                        for qt in range(QT):
                            weigh(oacc[:, qt, :], bank[:, qt, :], 1, qt)
                    if n == 10:
                        dve.wait_ge(cscore_done, l + 1)
                        csf = cs[:].rearrange("p a n -> p (a n)")
                        nc.vector.scalar_tensor_tensor(out=csf, in0=bank[:, 7, 0:QT * N_HEADS * NC], scalar=HEAD_DIM ** -0.5,
                                                       in1=calibi[:], op0=ALU.mult, op1=ALU.add).then_inc(cs_step, 1)
                        dve.wait_ge(cs_step, l * 5 + 1)
                        nc.vector.tensor_reduce(cmx[:], cs[:], AX.X, ALU.max).then_inc(cs_step, 1)
                        dve.wait_ge(cs_step, l * 5 + 2)
                        nc.vector.tensor_tensor(cs[:], cs[:], cmx[:].rearrange("p (a o) -> p a o", o=1).to_broadcast([P, QT * N_HEADS, NC]),
                                                ALU.subtract).then_inc(cs_step, 1)
                taps(TAPS)
                dve.wait_ge(ce_ready, l + 1)
                nc.vector.tensor_reduce(csum[:], ce[:], AX.X, ALU.add).then_inc(cs_step, 1)
                for qt in range(QT):
                    o = cp[:, qt].rearrange("p kv c n -> p c kv n")[:, :, :, 0:NC]
                    m = cok[:].rearrange("p (t c kv n) -> p t c kv n", t=QT, c=GROUP, kv=N_KV)[:, qt]
                    e = ce[:].rearrange("p (t c kv) n -> p t c kv n", t=QT, c=GROUP)[:, qt]
                    nc.vector.tensor_tensor(o, e, m, ALU.mult).then_inc(cp_ready, 1)
                dve.wait_ge(ysum_ready, l + 1)
                nc.vector.tensor_scalar(mu[:], bank[:, 0, 0:SEQ], 1.0 / CONV_CH, None, ALU.mult).then_inc(mu_ready, 1)
                dve.wait_ge(mu_ready, l + 1)
                nc.vector.tensor_tensor(yc[:], y[:], mu[:].rearrange("p (o t) -> p o t", o=1).to_broadcast([P, CT, SEQ]),
                                        ALU.subtract).then_inc(yc_ready, 1)
                dve.wait_ge(probs, l * N_JOBS + 12)
                factors(2, rsum[:, 1], gsel[:, :, 2, :], 2)
                dve.wait_ge(pv_done, l * N_JOBS + 12)
                for qt in range(QT):
                    weigh(otmp[:, 0, qt, :], bank[:, 2 + qt, :], 2, qt)
                dve.wait_ge(cs_step, l * 5 + 4)
                nc.vector.tensor_copy(cmx[:].rearrange("p (t kv c) -> p t kv c", t=QT, kv=N_KV),
                                      csum[:].rearrange("p (t c kv) -> p t kv c", t=QT, kv=N_KV)).then_inc(cs_step, 1)
                dve.wait_ge(cs_step, l * 5 + 5)
                factors(0, cmx[:].rearrange("p (t h) -> p t h", t=QT), gsel[:, :, 0, :], 4)
                dve.wait_ge(cpv_done, l + 1)
                for qt in range(QT):
                    weigh(otmp[:, 1, qt, :], bank[:, 4 + qt, :], 0, qt)
                dve.wait_ge(o_step, l * 10 + 4)
                for qt in range(QT):
                    nc.vector.tensor_tensor(oacc[:, qt], oacc[:, qt], otmp[:, 0, qt], ALU.add).then_inc(o_step, 1)
                for qt in range(QT):
                    dve.wait_ge(o_step, l * 10 + 7 + qt)
                    nc.vector.tensor_tensor(oacc[:, qt], oacc[:, qt], otmp[:, 1, qt], ALU.add).then_inc(o_step, 1)
                dve.wait_ge(ystd_ready, l + 1)
                nc.vector.reciprocal(yrstd[:], ystd[:]).then_inc(yrstd_ready, 1)
                dve.wait_ge(yrstd_ready, l + 1)
                for b in range(2):
                    dve.wait_ge(ah_ready, l * 2 + b + 1)
                    nc.vector.tensor_tensor(al[:, 2 * b:2 * b + 2, :].rearrange("p a t -> p (a t)"), bank[:, 6 + b, :],
                                            f32(ah[:, 2 * b:2 * b + 2, :]).rearrange("p a t -> p (a t)"),
                                            ALU.subtract).then_inc(al_ready, 1)
                nc.vector.tensor_tensor(yn[:], yc[:], yrstd[:].rearrange("p (o t) -> p o t", o=1).to_broadcast([P, CT, SEQ]),
                                        ALU.mult).then_inc(yn_ready, 1)
                for t in range(CT):
                    dve.wait_ge(ch_ready, l * CT + (t + 1))
                    nc.vector.tensor_tensor(cl[:, t, :], cz[:, t, :], f32(ch[:, t, :]), ALU.subtract).then_inc(cl_ready, 1)
                for u in range(U_OUT, MIX_UNITS - 1):
                    lo(l, MIX0 + u + RING)
                residual(l * 12 + 4, 1.0)

                scaled_low(l * 24 + 16, cur[:, C_N2:C_N2 + KT])
                lo(l, FFN2_0 - 1 + RING)
                recip(l * 3 + 2)
                ffn(l, 1)
                residual(l * 12 + 8, 0.5)
            recip(DEPTH * 3)
            for k in range(KT):
                normed(k, table[:, DEPTH * LAYER_COLS:])

        @block.tensor
        def _(pe):
            mm = nc.tensor.matmul

            def parts(o, n, col, width, a_hi, a_lo, start, stop, more=False):
                s = n % RING
                wh, wl = whi[:, s, col:col + width], wlo[:, s, col:col + width]
                mm(o, wh, a_hi, start=start, stop=False, skip_group_check=more)
                mm(o, wh, a_lo, start=False, stop=False, skip_group_check=more)
                return mm(o, wl, a_hi, start=False, stop=stop, skip_group_check=more)

            def sum_squares(q, q4, to):
                for b in range(4):
                    pe.wait_ge(sq_ready, q4 + (b + 1))
                    for k in (2 * b, 2 * b + 1):
                        m = mm(bank[:, to, 0:SEQ], ones[:], sq[:, k, :], start=(k == 0), stop=(k == KT - 1))
                m.then_inc(ssum_ready, 1)

            def split(at):
                pe.wait_ge(lo_ready, at)

            def project(n, o, width=P, x_from=None):
                for k in range(KT):
                    if x_from is not None:
                        pe.wait_ge(xl_ready, x_from + (k + 1))
                    m = parts(o, n, k * width, width, xh[:, k, :], xl[:, k, :], k == 0, k == KT - 1)
                m.then_inc(unit_used, 1)

            def to_residual(n, a_hi, a_lo, first, last):
                for m8 in range(KT):
                    m = parts(bank[:, m8 // 2, (m8 % 2) * SEQ:(m8 % 2 + 1) * SEQ], n, m8 * P, P, a_hi, a_lo,
                              first and m8 % 2 == 0, last, more=True)
                    if last and m8 % 2 == 1:
                        if m8 == KT - 1:
                            m.then_inc(y_ready, 1)
                        else:
                            m.then_inc(y_ready, 1)
                return m

            def ffn(l, f, x8, q):
                base = FFN2_0 if f else 0
                L = LAYER_UNITS

                def gate_up(c, j=None):
                    n, b = base + unit_g(c), 4 + 2 * (c % 2)
                    at, ht = l * L + n, l * 2 * FC + (f * FC + c - 1)
                    if j is not None:
                        at, ht = at + j * RING, ht + j * 2
                    if c >= 2:
                        pe.wait_ge(hid_ready, ht)
                    split(at + 1)
                    project(n, bank[:, b, 0:SEQ], x_from=x8 if c == 0 else None)
                    if c == 0:
                        sum_squares(q, q * 4, 0)
                    split(at + 2)
                    project(n + 1, bank[:, b + 1, 0:SEQ])

                def down(c, j=None):
                    n = base + unit_d(c)
                    at, ht = l * L + n, l * 2 * FC + (f * FC + c + 1)
                    if j is not None:
                        at, ht = at + j * RING, ht + j * 2
                    pe.wait_ge(hl_ready, ht)
                    split(at + 1)
                    m = to_residual(n, hh[:, c % 2, :], hl[:, c % 2, :], c == 0, c == FC - 1)
                    if c < FC - 1:
                        m.then_inc(unit_used, 1)

                gate_up(0)
                gate_up(1)
                down(0)
                with pe.Fori(0, (FC - 4) // 2) as j:
                    for c in (2, 3):
                        gate_up(c, j)
                        down(c - 1, j)
                gate_up(FC - 2)
                down(FC - 3)
                gate_up(FC - 1)
                down(FC - 2)
                down(FC - 1)
                last_unit()

            def last_unit():
                mm(bank[0:1, 6, 0:1], ones[:, 0:1], ones[:, 0:1], start=True, stop=True).then_inc(unit_used, 1)

            pe.wait_ge(setup_done, SETUP)
            pe.wait_ge(setup_done, SETUP)
            with pe.Fori(0, DEPTH) as l:
                ffn(l, 0, l * 24, l * 3)
                sum_squares(l * 3 + 1, l * 12 + 4, 7)

                def used(u):
                    split(l * LAYER_UNITS + (MIX0 + u + 1))

                for t in range(CT):
                    if t >= 2:
                        pe.wait_ge(glu_ready, l * CT + (t - 1))
                    for i in range(2):
                        used(2 * t + i)
                        project(MIX0 + 2 * t + i, bank[:, 4 + 2 * (t % 2) + i, 0:SEQ],
                                x_from=l * 24 + 8 if t == 0 and i == 0 else None)
                pe.wait_ge(glu_ready, l * CT + 3)
                for i in range(2):
                    used(U_KC + i)
                    project(MIX0 + U_KC + i, bank[:, 4 + i, 0:SEQ])
                pe.wait_ge(glu_ready, l * CT + 4)
                for i in range(2):
                    used(U_KS + i)
                    project(MIX0 + U_KS + i, bank[:, 6 + i, 0:SEQ])
                for c in range(GROUP):
                    used(U_Q + c)
                    project(MIX0 + U_Q + c, bank[:, c, 0:SEQ])
                pe.wait_ge(kk_ready, l * 8 + 8)
                for i in range(2):
                    used(U_V + i)
                    s = (MIX0 + U_V + i) % RING
                    for k4 in range(4):
                        k = 4 * i + k4
                        for t in range(QT):
                            xs = slice(t * P, (t + 1) * P)
                            wv = slice(k4 * 2 * P, (k4 + 1) * 2 * P)
                            o = bank[:, 4 + t, 0:2 * P]
                            mm(o, xh[:, k, xs], whi[:, s, wv], start=(k == 0), stop=False)
                            mm(o, xl[:, k, xs], whi[:, s, wv], start=False, stop=False)
                            m = mm(o, xh[:, k, xs], wlo[:, s, wv], start=False, stop=(k == KT - 1))
                    m.then_inc(unit_used, 1)
                pe.wait_ge(kz_ready, l * 4 + 4)
                used(U_GATE)
                project(MIX0 + U_GATE, bank[0:24, 6, 0:SEQ], width=24)

                def compress(n):
                    i, b = divmod(n, 4)
                    if b == 0:
                        pe.wait_ge(fl_ready, l * 2 + i + 1)
                        if i == 1:
                            pe.wait_ge(chid_ready, l * 2 + 1)
                    used(U_W1K + n)
                    s = (MIX0 + U_W1K + n) % RING
                    o = bank[0:N_KV * NC, 7, 0:2 * P]
                    for k4 in range(4):
                        k = 4 * b + k4
                        wv = slice(k4 * 2 * P, (k4 + 1) * 2 * P)
                        mm(o, fh[:, i, k, :], whi[:, s, wv], start=(k == 0), stop=False)
                        mm(o, fl[:, i, k, :], whi[:, s, wv], start=False, stop=False)
                        m = mm(o, fh[:, i, k, :], wlo[:, s, wv], start=False, stop=(k == 15))
                    m.then_inc(unit_used, 1)

                nb = N_KV * NC

                def turn_hidden():
                    used(U_W2)
                    pe.wait_ge(chid_ready, l * 2 + 2)
                    pe.wait_ge(gT_ready, l + 1)
                    for i in range(4):
                        m = mm(bank[:, 7, i * nb:(i + 1) * nb], chid[:, i // 2, (i % 2) * P:(i % 2 + 1) * P], ident[0:nb, 0:nb],
                               start=True, stop=True, skip_group_check=True)
                    m.then_inc(unit_used, 1)
                    for t in range(QT):
                        m = mm(bank[:, 7, 128 + t * 24:128 + (t + 1) * 24], gT[:, t * P:(t + 1) * P], ident[0:24, 0:24],
                               start=True, stop=True, skip_group_check=True)
                    m.then_inc(chid_turned, 1)

                def compress_out():
                    pe.wait_ge(w2_ready, l + 1)
                    pe.wait_ge(chidT_ready, l + 1)
                    pe.wait_ge(gate_ready, l + 1)
                    for kt in range(2):
                        mm(bank[:, 7, 0:nb], w2[:, kt * P:(kt + 1) * P], chidT[:, kt * nb:(kt + 1) * nb],
                           start=(kt == 0), stop=(kt == 1), skip_group_check=True)
                    for kv in range(N_KV):
                        for kt in range(2):
                            m = mm(bank[0:NC, 7, 64 + 64 * kv:128 + 64 * kv],
                                   chidT[:, (2 + kt) * nb + kv * NC:(2 + kt) * nb + (kv + 1) * NC],
                                   w2[:, 256 + 64 * kt:320 + 64 * kt], start=(kt == 0), stop=(kt == 1), skip_group_check=True)
                    m.then_inc(cmpkv_done, 1)

                def compressed_scores():
                    pe.wait_ge(cmpkv_ready, l * 10 + 10)
                    for t in range(QT):
                        for c in range(GROUP):
                            a = (t * GROUP + c) * nb
                            m = mm(bank[:, 7, a:a + nb], qT[:, c, t * P:(t + 1) * P], kcz[:].rearrange("p a n -> p (a n)"),
                                   start=True, stop=True, skip_group_check=True)
                    m.then_inc(cscore_done, 1)

                def scores(n):
                    br, qt, segs = job(n)
                    if n >= 2:
                        pe.wait_ge(scored, l * N_JOBS + (n - 1))
                    if qt == 1:
                        m = mm(bank[:, 4 + n % 2, :], qT[:, segs[0][0], P:2 * P], kz[:, br].rearrange("p a t -> p (a t)"),
                               start=True, stop=True)
                    else:
                        for i in range(2):
                            m = mm(bank[:, 4 + n % 2, 2 * P * i:2 * P * (i + 1)], qT[:, segs[2 * i][0], 0:P], kz[:, br, :, 0:P],
                                   start=True, stop=True, skip_group_check=True)
                    m.then_inc(scores_done, 1)

                def turn(n):
                    pe.wait_ge(probs, l * N_JOBS + (n + 1))
                    if n >= 1:
                        pe.wait_ge(prT_ready, l * N_JOBS + n)
                    for i in range(4):
                        m = nc.tensor.transpose(bank[:, 6, i * P:(i + 1) * P], pr[:, n % 2, i * P:(i + 1) * P], ident[:])
                    m.then_inc(turned, 1)

                def values(n):
                    br, qt, segs = job(n)
                    pe.wait_ge(prT_ready, l * N_JOBS + (n + 1))
                    at = 0
                    for h, kb in segs:
                        kv = h // GROUP
                        for b in range(kb):
                            m = mm(bank[:, 2 * br + qt, h * HEAD_DIM:(h + 1) * HEAD_DIM], prT[:, n % 2, at:at + P],
                                   v[:, b, br * P + kv * 64:br * P + kv * 64 + 64],
                                   start=(b == 0 and segs[0][0] == 0 and h == 0), stop=(b == kb - 1), skip_group_check=True)
                            at += P
                    m.then_inc(pv_done, 1)

                pe.wait_ge(q_ready, l * 4 + 4)
                pe.wait_ge(v_ready, l * 2 + 2)
                scores(0)
                scores(1)
                pe.wait_ge(consts_in, 16 * 4)
                pe.wait_ge(gT_ready, l + 1)
                for n in range(N_JOBS):
                    turn(n)
                    if n + 2 < N_JOBS:
                        scores(n + 2)
                    if n < 8:
                        compress(n)
                    if n == 8:
                        turn_hidden()
                    if n == 9:
                        compress_out()
                    if n == 10:
                        compressed_scores()
                    values(n)
                pe.wait_ge(tap_done, l * TAPS + TAPS)
                pe.wait_ge(o_step, l * 10 + 2)
                for t in range(CT):
                    m = mm(bank[:, 0, 0:SEQ], ones[:], y[:, t, :], start=(t == 0), stop=(t == CT - 1))
                m.then_inc(ysum_ready, 1)
                pe.wait_ge(cp_ready, l * 2 + 2)
                for i in range(QT * N_KV):
                    m = nc.tensor.transpose(bank[:, 6, i * P:(i + 1) * P],
                                            cp[:, i // N_KV, i % N_KV].rearrange("p c n -> p (c n)"), ident[:])
                m.then_inc(cp_turned, 1)
                pe.wait_ge(ysq_ready, l + 1)
                for t in range(CT):
                    m = mm(bank[:, 1, 0:SEQ], ones[:], ysq[:, t, :], start=(t == 0), stop=(t == CT - 1))
                m.then_inc(yvar_ready, 1)
                pe.wait_ge(cpT_ready, l + 1)
                for i in range(QT * N_KV):
                    t, kv = divmod(i, N_KV)
                    m = mm(bank[:, 4 + t, kv * 256:(kv + 1) * 256], cpT[:, t, kv, :], vcd[:, kv, :], start=True, stop=True,
                           skip_group_check=True)
                m.then_inc(cpv_done, 1)
                pe.wait_ge(o_step, l * 10 + 10)
                for t in range(4):
                    for qt in range(QT):
                        m = nc.tensor.transpose(bank[:, 6 + t // 2, (t % 2) * SEQ + qt * P:(t % 2) * SEQ + (qt + 1) * P],
                                                oacc[:, qt, t * P:(t + 1) * P], ident[:])
                m.then_inc(o_turned, 1)
                pe.wait_ge(ystd_ready, l + 1)
                for t in range(4):
                    used(U_OUT + t)
                    pe.wait_ge(al_ready, l * 2 + t // 2 + 1)
                    to_residual(MIX0 + U_OUT + t, ah[:, t, :], al[:, t, :], t == 0, False).then_inc(unit_used, 1)
                for t in range(CT):
                    used(U_OUT + 4 + t)
                    pe.wait_ge(cl_ready, l * CT + t + 1)
                    m = to_residual(MIX0 + U_OUT + 4 + t, ch[:, t, :], cl[:, t, :], False, t == 3)
                    if t < 3:
                        m.then_inc(unit_used, 1)
                last_unit()
                ffn(l, 1, l * 24 + 16, l * 3 + 2)
            sum_squares(DEPTH * 3, DEPTH * 12, 7)


def _columns(wt, cols):
    import numpy as np
    a = wt[:, cols].reshape(-1, 128, len(cols)).transpose(1, 0, 2).reshape(128, -1)
    u = np.zeros((128, 1024), np.float32)
    u[:, :a.shape[1]] = a
    return u


def _stream(a):
    import numpy as np
    units = []
    for l in range(2):
        def ffn(g, u, d):
            g, u, d = a[g][l], a[u][l], a[d][l]
            def gu(c):
                cols = np.arange(c * 128, (c + 1) * 128)
                units.append(_columns(g, cols))
                units.append(_columns(u, cols))
            gu(0)
            for c in range(1, 22):
                gu(c)
                units.append(d[(c - 1) * 128:c * 128])
            units.append(d[21 * 128:])
        ffn("ffn1_w_gate", "ffn1_w_up", "ffn1_w_down")
        w = a["w_in"][l]
        q0, kc, vc, ks, vs, kw, vw, gl, ga, gb = np.cumsum([0, 512, 128, 128, 128, 128, 128, 128, 24, 512])
        r = np.arange
        for t in range(4):
            units.append(_columns(w, gb + t * 128 + r(128)))
            units.append(_columns(w, ga + t * 128 + r(128)))
        for o in (kc, vc, ks, kw):
            units.append(_columns(w, o + r(128)))
        for c in range(4):
            units.append(_columns(w, np.concatenate([q0 + c * 64 + r(64), q0 + (c + 4) * 64 + r(64)])))
        vv = np.concatenate([vs + r(128), vw + r(128)])
        units.append(_columns(w[:512], vv))
        units.append(_columns(w[512:], vv))
        units.append(_columns(w, gl + np.array([h * 3 + b for b in range(3) for h in range(8)])))
        for n in ("cmp_k_w1", "cmp_v_w1"):
            for b in range(4):
                units.append(_columns(a[n][l][b * 512:(b + 1) * 512], r(256)))
        u = np.zeros((128, 1024), np.float32)
        for kt in range(2):
            k2 = a["cmp_k_w2"][l][kt * 128:(kt + 1) * 128]
            u[:, kt * 128:kt * 128 + 64] = k2
            u[:, kt * 128 + 64:kt * 128 + 128] = k2
            u[:, 256 + kt * 64:320 + kt * 64] = a["cmp_v_w2"][l][kt * 128:(kt + 1) * 128]
        units.append(u)
        for t in range(8):
            units.append(a["w_out"][l][t * 128:(t + 1) * 128])
        ffn("ffn2_w_gate", "ffn2_w_up", "ffn2_w_down")
    return np.stack(units)


def _params(a):
    import numpy as np
    cols = []
    tile = lambda vec: vec.reshape(-1, 128)
    for l in range(2):
        for n in ("ffn1_norm", "mix_norm", "ffn2_norm", "conv_b", "conv_norm_g", "conv_norm_b"):
            cols.append(tile(a[n][l]))
        cols.append(tile(a["conv_w"][l]))
        cols.append(tile(a["cmp_pos_k"][l]))
        cols.append(tile(a["cmp_pos_v"][l]))
    cols.append(tile(a["final_norm"]))
    return np.ascontiguousarray(np.concatenate(cols).T)


def _tables():
    import numpy as np
    slope = 2.0 ** (-8.0 * np.arange(1, 9) / 8)
    q, k = np.arange(128)[:, None], np.arange(256)[None]
    d = 128 + q - k
    bias = np.where(d[:, None, :] >= 0, -8.0 * slope[None, :, None] * d[:, None, :], -1e31).astype(np.float32)
    t = (np.arange(2)[None, :, None] * 128 + np.arange(128)[:, None, None])
    end = (np.arange(15) * 16 + 31)[None, None, :]
    dc = t - end
    sl = slope.reshape(2, 4).T.reshape(8)
    full = np.broadcast_to(dc[:, :, None, :], (128, 2, 8, 15))
    cb = np.where(full >= 0, -sl[None, None, :, None] * full, -1e30).astype(np.float32).reshape(128, 240)
    ok = (full >= 0).astype(np.float32).reshape(128, 240)
    return np.ascontiguousarray(bias), np.ascontiguousarray(cb), np.ascontiguousarray(ok)


def kernel(**inputs):
    import numpy as np
    import concourse.bacc as bacc
    from concourse.bass_utils import run_bass_kernel_spmd

    a = {k: np.asarray(v) for k, v in inputs.items()}
    bias, cb, ok = _tables()
    xT = np.ascontiguousarray(a["x"][0].T.reshape(8, 128, 256).transpose(1, 0, 2))
    arrays = {"w": _stream(a), "xT": xT, "params": _params(a), "bias": bias, "cbias": cb, "cmask": ok,
              "eye": np.eye(128, dtype=np.float32)}
    nc = bacc.Bacc("TRN2", target_bir_lowering=False, num_devices=1)
    aps = [nc.dram_tensor(n, v.shape, F32, kind="ExternalInput").ap() for n, v in arrays.items()]
    out = nc.dram_tensor("outT", (128, 8, 256), F32, kind="ExternalOutput").ap()
    trunk(nc, *aps, out)
    r = run_bass_kernel_spmd(nc, [arrays], core_ids=[0])
    o = r.results[0]["outT"]
    return np.ascontiguousarray(o.transpose(1, 0, 2).reshape(1024, 256).T)[None]
```

```python
import concourse.bass as bass
from concourse import mybir

F32 = mybir.dt.float32
F32R = mybir.dt.float32r
ALU = mybir.AluOpType
ACT = mybir.ActivationFunctionType
AX = mybir.AxisListType

P = 128
D_MODEL, SEQ, DEPTH = 1024, 256, 2
N_HEADS, HEAD_DIM, N_KV = 8, 64, 2
GROUP = N_HEADS // N_KV
D_FF = 2816
CONV_CH, CONV_WIDTH = 512, 31
PAD = CONV_WIDTH - 1
CMP_BLOCK, CMP_STRIDE = 32, 16
NC = SEQ // CMP_STRIDE - 1
EPS = 1e-6
BIG = 3.0e38

KT = D_MODEL // P
QT = SEQ // P
CT = CONV_CH // P
FC = D_FF // P
BANK = 512
UNIT = 1024
RING = 6

FFN_UNITS = 3 * FC
U_GLU, U_KC, U_VC, U_KS, U_KW, U_GATE, U_V, U_W1K, U_W1V, U_Q, U_W2, U_OUT = 0, 8, 9, 10, 11, 12, 13, 15, 19, 23, 27, 28
MIX_UNITS = 36
MIX0 = FFN_UNITS
FFN2_0 = MIX0 + MIX_UNITS
LAYER_UNITS = FFN2_0 + FFN_UNITS
DIRECT = [*range(MIX0 + U_GATE, MIX0 + U_Q), MIX0 + U_W2]
LAYER_SPLITS = LAYER_UNITS - len(DIRECT)
assert MIX0 % RING == 0 and FFN2_0 % RING == 0 and LAYER_UNITS % RING == 0

C_N1, C_NM, C_N2 = 0, KT, 2 * KT
C_CB = 3 * KT
C_CG = C_CB + CT
C_CBETA = C_CG + CT
C_CW = C_CBETA + CT
C_POS = C_CW + CONV_WIDTH * CT
LAYER_COLS = C_POS + 2 * (CMP_BLOCK // 2)

N_JOBS = 12
PR = 4
TAPS = CONV_WIDTH * CT
TAP_TILES = [(6, [0]), (6, [0, 1]), (12, [0, 1, 2])]
TAPS_PROJ = [0, 0, 3, 3, 3, 3, 6, 6, 6, 6, 4, 4, 3, 8, 8, 12, 12, 4, 2, 2, 2, 4, 2, 3, 2, 2, 3]
TAPS_JOB = [3, 2, 2, 2, 2]
JOB_CMP_SCORES, JOB_CMP_MASK, JOB_CMP_TURN, JOB_YSUM, JOB_YVAR, JOB_YNORM, JOB_SELECTED = 1, 3, 5, 7, 8, 10, 9
PRE_SCORES = {U_Q + 1: 0, U_Q + 2: 1}


def splits_to(n):
    return n + 1 - sum(d <= n for d in DIRECT)


def unit_g(c):
    return 0 if c == 0 else 2 + 3 * (c - 1)


def unit_d(c):
    return FFN_UNITS - 1 if c == FC - 1 else unit_g(c + 1) + 2


def job(n):
    br, m = divmod(n, 6)
    if m < 4:
        return br, 1, [(m, 2), (m + GROUP, 2)]
    g = 2 * (m - 4)
    return br, 0, [(g, 1), (g + GROUP, 1), (g + 1, 1), (g + 1 + GROUP, 1)]


def trunk(nc, w, xT, params, bias, cbias, cmask, eye, out):
    from contextlib import ExitStack
    ctx = ExitStack()
    with ctx:
        sb = lambda name, shape, dt=F32: ctx.enter_context(nc.sbuf_tensor(name, shape, dt))
        sem = lambda name: ctx.enter_context(nc.semaphore(name))
        bank = ctx.enter_context(nc.psum_tensor("bank", [P, 8, BANK], F32))

        raw = sb("raw", [P, RING, UNIT])
        whi = sb("whi", [P, RING, UNIT], F32R)
        wlo = sb("wlo", [P, RING, UNIT], F32R)
        x = sb("x", [P, KT, SEQ])
        sq = sb("sq", [P, KT, SEQ])
        xn = sb("xn", [P, KT, SEQ])
        xh = sb("xh", [P, KT, SEQ], F32R)
        xl = sb("xl", [P, KT, SEQ], F32R)
        std = sb("std", [P, SEQ])
        rstd = sb("rstd", [P, SEQ])
        sil = sb("sil", [P, 2, SEQ])
        up = sb("up", [P, 2, SEQ])
        hid = sb("hid", [P, 2, SEQ])
        hh = sb("hh", [P, 2, SEQ], F32R)
        hl = sb("hl", [P, 2, SEQ], F32R)
        table = sb("table", [P, DEPTH * LAYER_COLS + KT])
        cur = sb("cur", [P, LAYER_COLS])
        alibi = sb("alibi", [P, N_HEADS, 2 * P])
        calibi = sb("calibi", [P, QT * N_HEADS * NC])
        cok = sb("cok", [P, QT * N_HEADS * NC])
        ident = sb("ident", [P, P])
        ones = sb("ones", [P, P])
        eps = sb("eps", [P, 1])
        sig = sb("sig", [P, 2, SEQ])
        upad = sb("upad", [P, CT, PAD + SEQ])
        y = sb("y", [P, CT, SEQ])
        mu = sb("mu", [P, SEQ])
        yc = sb("yc", [P, CT, SEQ])
        ysq = sb("ysq", [P, CT, SEQ])
        ystd = sb("ystd", [P, SEQ])
        yrstd = sb("yrstd", [P, SEQ])
        yn, cz = ysq, yc
        qT = sb("qT", [P, GROUP, SEQ])
        kz = sb("kz", [P, 2, N_KV, SEQ])
        v = sb("v", [P, QT, 2 * P])
        gate = sb("gate", [P, QT, 24])
        kk = sb("kk", [P, 2, N_KV, SEQ])
        flat = sb("flat", [P, 2, CMP_BLOCK // 2, N_KV * NC])
        chid = sb("chid", [N_KV * NC, 2, 2 * P])
        chidT = sb("chidT", [P, 4 * N_KV * NC])
        kcz = sb("kcz", [P, N_KV, NC])
        vcd = sb("vcd", [P, N_KV, GROUP * HEAD_DIM])
        cs = sb("cs", [P, QT * N_HEADS, NC])
        cmx = sb("cmx", [P, QT * N_HEADS])
        ce = sb("ce", [P, QT * N_HEADS, NC])
        csum = sb("csum", [P, QT * N_HEADS])
        cp = sb("cp", [P, QT, N_KV, GROUP, 32])
        cpT = sb("cpT", [P, QT, N_KV, P])
        ch, ah = xh[:, 0:CT, :], xh[:, CT:KT, :]
        cl, al = xl[:, 0:CT, :], xl[:, CT:KT, :]
        pr = [b.rearrange("p a t -> p (a t)") for b in (xn[:, 0:2, :], xn[:, 2:4, :], kk[:, 0], kk[:, 1])]
        held = sb("held", [P, PR])
        nmax = sb("nmax", [P, PR, 4])
        prT = xn[:, 4:8, :].rearrange("p (b a) t -> p b (a t)", b=2)
        rsum = sb("rsum", [P, 2, QT, N_HEADS])
        rrec = sb("rrec", [P, 3, QT, N_HEADS])
        fac = sb("fac", [P, 3, QT, N_HEADS])
        oacc = sb("oacc", [P, QT, BANK])
        otmp = sq[:].rearrange("p (b t a) s -> p b t (a s)", b=2, t=QT)

        landed = [sem(f"landed{s}") for s in range(RING)]
        x_in = [sem(f"x_in{b}") for b in range(4)]
        table_in, consts_in, out_done = sem("table_in"), sem("consts_in"), sem("out_done")
        setup_done = sem("setup_done")
        cur_ready = sem("cur_ready")
        hi_ready, lo_ready, unit_used = sem("hi_ready"), sem("lo_ready"), sem("unit_used")
        x_ready, sq_ready, folded, ssum_ready = sem("x_ready"), sem("sq_ready"), sem("folded"), sem("ssum_ready")
        std_ready, rstd_ready = sem("std_ready"), sem("rstd_ready")
        xn_ready, xh_ready, xl_ready = sem("xn_ready"), sem("xh_ready"), sem("xl_ready")
        y_ready = sem("y_ready")
        gn_ready, un_ready = sem("gn_ready"), sem("un_ready")
        sil_ready, hid_ready, hh_ready, hl_ready = sem("sil_ready"), sem("hid_ready"), sem("hh_ready"), sem("hl_ready")
        sig_ready, glu_ready, tap_done = sem("sig_ready"), sem("glu_ready"), sem("tap_done")
        ysum_ready, mu_ready, yc_ready, ysq_ready = sem("ysum_ready"), sem("mu_ready"), sem("yc_ready"), sem("ysq_ready")
        yvar_ready, ystd_ready, yrstd_ready, yn_ready = sem("yvar_ready"), sem("ystd_ready"), sem("yrstd_ready"), sem("yn_ready")
        cz_ready, ch_ready, cl_ready = sem("cz_ready"), sem("ch_ready"), sem("cl_ready")
        kk_ready, kz_ready, q_ready, v_ready = sem("kk_ready"), sem("kz_ready"), sem("q_ready"), sem("v_ready")
        gate_ready = sem("gate_ready")
        flat_ready = sem("flat_ready")
        chid_ready, chid_turned, chidT_ready = sem("chid_ready"), sem("chid_turned"), sem("chidT_ready")
        cmpkv_ready, cscore_done = sem("cmpkv_ready"), sem("cscore_done")
        cs_step, ce_ready, cp_ready, cp_turned, cpT_ready, cpv_done = (
            sem("cs_step"), sem("ce_ready"), sem("cp_ready"), sem("cp_turned"), sem("cpT_ready"), sem("cpv_done"))
        scores_done, scored, probs, turned, prT_ready, pv_done = (
            sem("scores_done"), sem("scored"), sem("probs"), sem("turned"), sem("prT_ready"), sem("pv_done"))
        fac_step, o_step, o_turned, ah_ready, al_ready = (
            sem("fac_step"), sem("o_step"), sem("o_turned"), sem("ah_ready"), sem("al_ready"))

        block = ctx.enter_context(nc.Block())
        f32 = lambda ap: ap.bitcast(F32)

        @block.sync
        def _(sp):
            sp.dma_start(table[:], params).then_inc(table_in, 16)
            for b in range(4):
                sp.dma_start(xn[:, 2 * b:2 * b + 2, :], xT[:, 2 * b:2 * b + 2, :]).then_inc(x_in[b], 16)
                if b == 0:
                    sp.dma_start(raw[:, 0, :], w[0]).then_inc(landed[0], 16)
            for s in range(1, RING):
                sp.dma_start(raw[:, s, :], w[s]).then_inc(landed[s], 16)
            sp.dma_start(ident[:], eye).then_inc(consts_in, 16)
            sp.dma_start(alibi[:], bias).then_inc(consts_in, 16)
            sp.dma_start(calibi[:], cbias).then_inc(consts_in, 16)
            sp.dma_start(cok[:], cmask).then_inc(consts_in, 16)
            def refill(l, n, j=None):
                rounds = 0 if j is None else j * RING
                if n in DIRECT:
                    sp.wait_ge(unit_used, l * LAYER_UNITS + (n + 1))
                else:
                    sp.wait_ge(lo_ready, l * LAYER_SPLITS + rounds + splits_to(n))
                sp.dma_start(raw[:, n % RING, :], w[l * LAYER_UNITS + rounds + (n + RING)]).then_inc(landed[n % RING], 16)

            def layer(l):
                with sp.Fori(0, MIX0 // RING) as j:
                    for n in range(RING):
                        refill(l, n, j)
                for n in range(MIX0, FFN2_0):
                    refill(l, n)
                with sp.Fori(0, FFN_UNITS // RING - 1) as j:
                    for n in range(FFN2_0, FFN2_0 + RING):
                        refill(l, n, j)

            with sp.Fori(0, DEPTH - 1) as l:
                layer(l)
                for n in range(LAYER_UNITS - RING, LAYER_UNITS):
                    refill(l, n)
            layer(DEPTH - 1)
            for k in range(KT):
                sp.wait_ge(xn_ready, DEPTH * KT + k + 1)
                sp.dma_start(out[:, k, :], xn[:, k, :]).then_inc(out_done, 16)
            sp.wait_ge(out_done, 16 * KT)

        @block.gpsimd
        def _(pool):
            nc.gpsimd.memset(upad[:, :, 0:PAD], 0.0).then_inc(setup_done, 1)
            nc.gpsimd.memset(kz[:], 0.0).then_inc(setup_done, 1)
            nc.gpsimd.memset(kcz[:], 0.0).then_inc(setup_done, 1)
            nc.gpsimd.memset(vcd[:], 0.0).then_inc(setup_done, 1)
            nc.gpsimd.memset(cp[:], 0.0).then_inc(setup_done, 1)
            nc.gpsimd.memset(ones[:], 1.0).then_inc(setup_done, 1)
            nc.gpsimd.memset(eps[:], EPS).then_inc(setup_done, 1)

        SETUP = 7

        @block.scalar
        def _(act):
            def hi(l, n):
                if n in DIRECT:
                    return
                act.wait_ge(landed[n % RING], l * (16 * LAYER_UNITS // RING) + 16 * (n // RING + 1))
                if n >= RING:
                    act.wait_ge(unit_used, l * LAYER_UNITS + (n - RING + 1))
                nc.scalar.copy(whi[:, n % RING, :], raw[:, n % RING, :]).then_inc(hi_ready, 1)

            def hi_in_loop(l, j, n):
                act.wait_ge(landed[n % RING], l * (16 * LAYER_UNITS // RING) + j * 16 + 16 * (n // RING + 1))
                act.wait_ge(unit_used, l * LAYER_UNITS + j * RING + (n - RING + 1))
                nc.scalar.copy(whi[:, n % RING, :], raw[:, n % RING, :]).then_inc(hi_ready, 1)

            def square(q4, b):
                act.wait_ge(x_ready, q4 + (b + 1))
                nc.scalar.activation(sq[:, 2 * b:2 * b + 2, :], x[:, 2 * b:2 * b + 2, :], ACT.Square).then_inc(sq_ready, 1)

            def root(q, src):
                act.wait_ge(ssum_ready, q + 1)
                nc.scalar.activation(std[:], src, ACT.Sqrt, scale=1.0 / D_MODEL, bias=eps[:, 0:1]).then_inc(std_ready, 1)

            def scaled_high(l, q4, x8, gains):
                act.wait_ge(cur_ready, l + 1)
                for k in range(KT):
                    if k % 2 == 0:
                        act.wait_ge(x_ready, q4 + (k // 2 + 1))
                    nc.scalar.mul(xh[:, k, :], x[:, k, :], gains[:, k:k + 1]).then_inc(xh_ready, 1)

            def high_x(x8, n8):
                for k in range(KT):
                    act.wait_ge(xn_ready, n8 + (k + 1))
                    nc.scalar.copy(xh[:, k, :], xn[:, k, :]).then_inc(xh_ready, 1)

            def silu(l, f, j, c):
                act.wait_ge(gn_ready, l * 2 * FC + j * 2 + (f * FC + c + 1))
                nc.scalar.activation(sil[:, c % 2, :], sil[:, c % 2, :], ACT.Silu).then_inc(sil_ready, 1)

            def ffn(l, f):
                base = FFN2_0 if f else 0

                def steps(c, j=None):
                    for i, n in enumerate(range(unit_g(c), min(unit_g(c + 1), FFN_UNITS - 1))):
                        if c == 0 and i == 0:
                            silu(l, f, 0, 0)
                            hi(l, base + RING - 1)
                        if base + n + RING < LAYER_UNITS and (c < FC - 1 or i == 0):
                            if j is None:
                                hi(l, base + n + RING)
                            else:
                                hi_in_loop(l, j, base + n + RING)
                        if c > 0 and i == 0:
                            silu(l, f, 0 if j is None else j, c)

                steps(0)
                steps(1)
                with act.Fori(0, (FC - 4) // 2) as j:
                    steps(2, j)
                    steps(3, j)
                steps(FC - 2)
                steps(FC - 1)
                nc.scalar.preload_act_table(ACT.Sqrt)

            def head(l, early):
                for n in range(early):
                    hi(l, n)
                scaled_high(l, l * 12, l * 24, cur[:, C_N1:C_N1 + KT])
                for n in range(early, 2):
                    hi(l, n)
                for b in range(4):
                    square(l * 12, b)

            def layer(l, early):
                if early < 3:
                    hi(l, 2)
                hi(l, 3)
                root(l * 3, bank[:, 0, 0:SEQ])
                nc.scalar.preload_act_table(ACT.Silu)
                hi(l, 4)
                ffn(l, 0)

                for b in range(4):
                    square(l * 12 + 4, b)
                for n in range(MIX0 - 3, MIX0):
                    hi(l, n + RING)
                root(l * 3 + 1, bank[:, 7, 0:SEQ])
                nc.scalar.preload_act_table(ACT.Sigmoid)
                high_x(l * 24 + 8, l * 8)

                def done(u):
                    act.wait_ge(unit_used, l * LAYER_UNITS + (MIX0 + u + 1))

                def exps(n):
                    br, qt, segs = job(n)
                    act.wait_ge(scored, l * N_JOBS + (n + 1))
                    at = 0
                    for i, (h, kb) in enumerate(segs):
                        p = pr[n % PR][:, at:at + P * kb]
                        e = nc.scalar.activation(p, p, ACT.Exp, scale=-1.0, bias=nmax[:, n % PR, i:i + 1],
                                                 accum_out=rsum[:, br, qt, h:h + 1])
                        at += P * kb
                    e.then_inc(probs, 1)

                def copy_prT(n):
                    act.wait_ge(turned, l * N_JOBS + (n + 1))
                    if n >= 2:
                        act.wait_ge(pv_done, l * N_JOBS + (n - 1))
                    nc.scalar.copy(prT[:, n % 2, :], bank[:, 6, :]).then_inc(prT_ready, 1)

                for u in range(U_W2):
                    done(u)
                    if u < U_KC and u % 2 == 0:
                        t = u // 2 % 2
                        nc.scalar.activation(sig[:, t, :], bank[:, 4 + 2 * t, 0:SEQ], ACT.Sigmoid).then_inc(sig_ready, 1)
                    if u in (U_KC, U_VC):
                        i = u - U_KC
                        for kv in range(N_KV):
                            src = bank[64 * kv:64 * kv + 64, i, :]
                            nc.scalar.copy(kk[0:64, i, kv, :], src[:, 0:SEQ]).then_inc(kk_ready, 1)
                            nc.scalar.copy(kk[64:128, i, kv, 0:SEQ - 1], src[:, 1:SEQ]).then_inc(kk_ready, 1)
                    if u in (U_KS, U_KW):
                        i = u - U_KS
                        for kv in range(N_KV):
                            r = slice(64 * kv, 64 * kv + 64)
                            nc.scalar.copy(kz[r, i, kv, :], bank[r, 2 + i, 0:SEQ]).then_inc(kz_ready, 1)
                    if u == U_GATE:
                        nc.scalar.activation(gate[:], bank[:, 6, 0:QT * 24].rearrange("p (t g) -> p t g", t=QT),
                                             ACT.Sigmoid).then_inc(gate_ready, 1)
                        nc.scalar.preload_act_table(ACT.Silu)
                    if u == U_V + 1:
                        for t in range(QT):
                            nc.scalar.copy(v[:, t, :], bank[:, 4 + t, 0:SEQ]).then_inc(v_ready, 1)
                    if u in (U_W1K + 3, U_W1V + 3):
                        i = (u - U_W1K) // 4
                        nc.scalar.activation(chid[:, i, :], bank[0:N_KV * NC, 7 - i, 0:2 * P], ACT.Silu).then_inc(chid_ready, 1)
                        if i == 1:
                            nc.scalar.preload_act_table(ACT.Exp)
                    if u >= U_Q:
                        nc.scalar.copy(qT[:, u - U_Q, :], bank[:, u - U_Q, 0:SEQ]).then_inc(q_ready, 1)
                    hi(l, MIX0 + u + RING)
                    if u == U_Q + 1:
                        act.wait_ge(chid_turned, l + 1)
                        nc.scalar.copy(chidT[:], bank[:, 7, 0:4 * N_KV * NC]).then_inc(chidT_ready, 1)
                    if u - 1 in PRE_SCORES:
                        exps(PRE_SCORES[u - 1])
                done(U_W2)
                for kv in range(N_KV):
                    r = slice(64 * kv, 64 * kv + 64)
                    nc.scalar.copy(kcz[r, kv, :], bank[r, 7, kv * NC:(kv + 1) * NC]).then_inc(cmpkv_ready, 1)
                for n in range(N_JOBS):
                    copy_prT(n)
                    if n == 0:
                        for kv in range(N_KV):
                            for g in range(GROUP):
                                nc.scalar.copy(vcd[32 * g:32 * g + NC, kv, g * HEAD_DIM:(g + 1) * HEAD_DIM],
                                               bank[0:NC, 7, 64 + 64 * kv:128 + 64 * kv]).then_inc(cmpkv_ready, 1)
                    if n + 2 < N_JOBS:
                        exps(n + 2)
                    if n == 4:
                        hi(l, MIX0 + U_W2 + RING)
                    if n == JOB_CMP_SCORES:
                        act.wait_ge(cs_step, l * 5 + 3)
                        nc.scalar.activation(ce[:], cs[:], ACT.Exp).then_inc(ce_ready, 1)
                    if n == JOB_CMP_TURN:
                        act.wait_ge(cp_turned, l + 1)
                        nc.scalar.copy(cpT[:].rearrange("p t k q -> p (t k q)"), bank[:, 7, :]).then_inc(cpT_ready, 1)
                    if n == N_JOBS - 3:
                        nc.scalar.preload_act_table(ACT.Sqrt)
                    if n == N_JOBS - 2:
                        act.wait_ge(yvar_ready, l + 1)
                        nc.scalar.activation(ystd[:], bank[:, 7, 0:SEQ], ACT.Sqrt, scale=1.0 / CONV_CH,
                                             bias=eps[:, 0:1]).then_inc(ystd_ready, 1)
                        nc.scalar.preload_act_table(ACT.Silu)
                for t in range(CT):
                    act.wait_ge(yn_ready, l * CT + (t + 1))
                    nc.scalar.activation(cz[:, t, :], yn[:, t, :], ACT.Silu, scale=cur[:, C_CG + t:C_CG + t + 1],
                                         bias=cur[:, C_CBETA + t:C_CBETA + t + 1]).then_inc(cz_ready, 1)
                    act.wait_ge(cz_ready, l * CT + (t + 1))
                    nc.scalar.copy(ch[:, t, :], cz[:, t, :]).then_inc(ch_ready, 1)
                for u in range(U_OUT, U_OUT + 2):
                    hi(l, MIX0 + u + RING)
                nc.scalar.preload_act_table(ACT.Sqrt)
                act.wait_ge(o_turned, l + 1)
                for b in range(2):
                    nc.scalar.copy(ah[:, 2 * b:2 * b + 2, :], bank[:, 6 + b, :]).then_inc(ah_ready, 1)
                for u in range(U_OUT + 2, MIX_UNITS - 1):
                    hi(l, MIX0 + u + RING)

                scaled_high(l, l * 12 + 8, l * 24 + 16, cur[:, C_N2:C_N2 + KT])
                for b in range(4):
                    square(l * 12 + 8, b)
                root(l * 3 + 2, bank[:, 0, 0:SEQ])
                nc.scalar.preload_act_table(ACT.Silu)
                ffn(l, 1)

            nc.scalar.preload_act_table(ACT.Sqrt)
            act.wait_ge(setup_done, SETUP)
            head(0, 1)
            with act.Fori(0, DEPTH - 1) as l:
                layer(l, 1)
                head(l + 1, 3)
            layer(DEPTH - 1, 3)
            for b in range(4):
                square(DEPTH * 12, b)
            root(DEPTH * 3, bank[:, 7, 0:SEQ])

        @block.vector
        def _(dve):
            def lo(l, n):
                if n in DIRECT:
                    return
                dve.wait_ge(hi_ready, l * LAYER_SPLITS + splits_to(n))
                nc.vector.tensor_tensor(wlo[:, n % RING, :], raw[:, n % RING, :], f32(whi[:, n % RING, :]),
                                        ALU.subtract).then_inc(lo_ready, 1)

            def lo_in_loop(l, j, n):
                dve.wait_ge(hi_ready, l * LAYER_SPLITS + j * RING + splits_to(n))
                nc.vector.tensor_tensor(wlo[:, n % RING, :], raw[:, n % RING, :], f32(whi[:, n % RING, :]),
                                        ALU.subtract).then_inc(lo_ready, 1)

            def take_gains(l):
                nc.vector.tensor_copy(cur[:], table[:, bass.ds(l * LAYER_COLS, LAYER_COLS)]).then_inc(cur_ready, 1)

            def residual(y4, scale, x8=None, gains=None):
                for b in range(4):
                    if gains is not None and b >= 2:
                        scaled_low(x8, gains, range(2 * b - 4, 2 * b - 2))
                    dve.wait_ge(y_ready, y4 + (b + 1))
                    xb = x[:, 2 * b:2 * b + 2, :].rearrange("p a t -> p (a t)")
                    nc.vector.scalar_tensor_tensor(out=xb, in0=bank[:, b, :], scalar=scale, in1=xb,
                                                   op0=ALU.mult, op1=ALU.add).then_inc(x_ready, 1)
                if gains is not None:
                    scaled_low(x8, gains, range(4, KT))

            def recip(q):
                dve.wait_ge(std_ready, q + 1)
                nc.vector.reciprocal(rstd[:], std[:]).then_inc(rstd_ready, 1)
                dve.wait_ge(rstd_ready, q + 1)

            def normed(k, gains):
                nc.vector.scalar_tensor_tensor(out=xn[:, k, :], in0=x[:, k, :], scalar=gains[:, k:k + 1],
                                               in1=rstd[:], op0=ALU.mult, op1=ALU.mult).then_inc(xn_ready, 1)

            def low_x(x8, k):
                dve.wait_ge(xh_ready, x8 + (k + 1))
                nc.vector.tensor_tensor(xl[:, k, :], xn[:, k, :], f32(xh[:, k, :]), ALU.subtract).then_inc(xl_ready, 1)

            def scaled_low(x8, gains, ks=range(KT)):
                for k in ks:
                    dve.wait_ge(xh_ready, x8 + (k + 1))
                    nc.vector.scalar_tensor_tensor(out=xl[:, k, :], in0=x[:, k, :], scalar=gains[:, k:k + 1],
                                                   in1=f32(xh[:, k, :]), op0=ALU.mult, op1=ALU.subtract).then_inc(xl_ready, 1)

            def gate_normed(l, f, j, c):
                dve.wait_ge(unit_used, l * LAYER_UNITS + j * RING + ((FFN2_0 if f else 0) + unit_g(c) + 1))
                b = c % 2
                nc.vector.tensor_tensor(sil[:, b, :], bank[:, 4 + 2 * b, 0:SEQ], rstd[:], ALU.mult).then_inc(gn_ready, 1)

            def hidden(l, f, j, c):
                h0 = f * FC + c + 1
                b = c % 2
                dve.wait_ge(unit_used, l * LAYER_UNITS + j * RING + ((FFN2_0 if f else 0) + unit_g(c) + 2))
                nc.vector.tensor_tensor(up[:, b, :], bank[:, 5 + 2 * b, 0:SEQ], rstd[:], ALU.mult).then_inc(un_ready, 1)
                dve.wait_ge(un_ready, l * 2 * FC + j * 2 + h0)
                dve.wait_ge(sil_ready, l * 2 * FC + j * 2 + h0)
                nc.vector.tensor_tensor(hid[:, b, :], up[:, b, :], sil[:, b, :], ALU.mult).then_inc(hid_ready, 1)
                dve.wait_ge(hid_ready, l * 2 * FC + j * 2 + h0)
                nc.vector.tensor_copy(hh[:, b, :], hid[:, b, :]).then_inc(hh_ready, 1)
                dve.wait_ge(hh_ready, l * 2 * FC + j * 2 + h0)
                nc.vector.tensor_tensor(hl[:, b, :], hid[:, b, :], f32(hh[:, b, :]), ALU.subtract).then_inc(hl_ready, 1)

            def fold(q, q4):
                dve.wait_ge(sq_ready, q4 + 4)
                for i, w in enumerate((4, 2)):
                    nc.vector.tensor_tensor(sq[:, 0:w, :], sq[:, 0:w, :], sq[:, w:2 * w, :], ALU.add).then_inc(folded, 1)
                    if w > 2:
                        dve.wait_ge(folded, q * 2 + 1)

            def ffn(l, f):
                base = FFN2_0 if f else 0

                def steps(c, j=None):
                    for i, n in enumerate(range(unit_g(c), min(unit_g(c + 1), FFN_UNITS - 1))):
                        if i == 0:
                            gate_normed(l, f, 0 if j is None else j, c)
                            if c == 0 and f == 0:
                                lo(l, 4)
                        if i == 1:
                            hidden(l, f, 0 if j is None else j, c)
                        if c == 0 and i == 0:
                            continue
                        if c == 0 and i == 1:
                            lo(l, base + RING - 1)
                            lo(l, base + RING)
                        if base + n + RING < LAYER_UNITS and (c < FC - 1 or i == 0):
                            if j is None:
                                lo(l, base + n + RING)
                            else:
                                lo_in_loop(l, j, base + n + RING)

                steps(0)
                steps(1)
                with dve.Fori(0, (FC - 4) // 2) as j:
                    steps(2, j)
                    steps(3, j)
                steps(FC - 2)
                steps(FC - 1)

            def layer(l, early):
                for n in range(early, 2):
                    lo(l, n)
                if early < 2:
                    fold(l * 2, l * 12)
                lo(l, 2)
                if early == 2:
                    fold(l * 2, l * 12)
                lo(l, 3)
                recip(l * 3)
                ffn(l, 0)
                residual(l * 12, 0.5)

                for n in (MIX0 - 3, MIX0 - 2):
                    lo(l, n + RING)
                recip(l * 3 + 1)
                for k in range(KT + 1):
                    if k < KT:
                        normed(k, cur[:, C_NM:C_NM + KT])
                    if k:
                        low_x(l * 24 + 8, k - 1)
                lo(l, MIX0 - 1 + RING)

                def done(u):
                    dve.wait_ge(unit_used, l * LAYER_UNITS + (MIX0 + u + 1))

                tap_order, left = [], [list(range(CONV_WIDTH)) for _ in range(CT)]
                for count, tiles in TAP_TILES:
                    for i in range(count):
                        t = tiles[i % len(tiles)]
                        if left[t]:
                            tap_order.append((left[t].pop(0), t))
                while any(left):
                    for t in range(CT):
                        if left[t]:
                            tap_order.append((left[t].pop(0), t))
                place = {jt: i for i, jt in enumerate(tap_order)}
                next_tap = [0]

                def taps(n):
                    for i in range(next_tap[0], min(next_tap[0] + n, TAPS)):
                        j, t = tap_order[i]
                        wj = cur[:, C_CW + j * CT + t:C_CW + j * CT + t + 1]
                        src = upad[:, t, j:j + SEQ]
                        if j == 0:
                            dve.wait_ge(glu_ready, l * CT + (t + 1))
                            nc.vector.tensor_scalar(y[:, t, :], src, wj, cur[:, C_CB + t:C_CB + t + 1],
                                                    ALU.mult, ALU.add).then_inc(tap_done, 1)
                        else:
                            dve.wait_ge(tap_done, l * TAPS + (place[j - 1, t] + 1))
                            nc.vector.scalar_tensor_tensor(out=y[:, t, :], in0=src, scalar=wj, in1=y[:, t, :],
                                                           op0=ALU.mult, op1=ALU.add).then_inc(tap_done, 1)
                    next_tap[0] = min(next_tap[0] + n, TAPS)

                def score(n):
                    br, qt, segs = job(n)
                    dve.wait_ge(scores_done, l * N_JOBS + (n + 1))
                    if n >= PR:
                        dve.wait_ge(turned, l * N_JOBS + (n - PR + 1))
                    nc.vector.memset(held[:, n % PR:n % PR + 1], 0.0)
                    at = 0
                    for i, (h, kb) in enumerate(segs):
                        s = nc.vector.tensor_tensor_reduce(
                            pr[n % PR][:, at:at + P * kb], bank[:, 4 + n % 2, at:at + P * kb], alibi[:, h, 2 * P - P * kb:],
                            -(HEAD_DIM ** -0.5), BIG, ALU.add, ALU.min, nmax[:, n % PR, i:i + 1])
                        at += P * kb
                    s.then_inc(scored, 1)

                def factors(b, sums, gates, k0):
                    nc.vector.reciprocal(rrec[:, b], sums).then_inc(fac_step, 1)
                    dve.wait_ge(fac_step, l * 6 + k0 + 1)
                    nc.vector.tensor_tensor(fac[:, b], rrec[:, b], gates, ALU.mult).then_inc(fac_step, 1)
                    dve.wait_ge(fac_step, l * 6 + k0 + 2)

                def weigh(dst, src, b, qt):
                    nc.vector.tensor_tensor(
                        dst.rearrange("p (h d) -> p h d", h=N_HEADS), src.rearrange("p (h d) -> p h d", h=N_HEADS),
                        fac[:, b, qt, :].rearrange("p (h o) -> p h o", o=1).to_broadcast([P, N_HEADS, HEAD_DIM]),
                        ALU.mult).then_inc(o_step, 1)

                for u in range(U_W2):
                    if u in (U_VC + 1, U_VC + 2):
                        i = u - U_VC - 1
                        dve.wait_ge(kk_ready, l * 8 + 4 * i + 4)
                        for kv in range(N_KV):
                            src = kk[:, i, kv, :].rearrange("p (n s) -> p s n", s=CMP_STRIDE)
                            for half in range(2):
                                a = src[:, 0:CMP_STRIDE:2, half:half + NC]
                                pos = cur[:, C_POS + 16 * i + 8 * half:C_POS + 16 * i + 8 * half + 8]
                                nc.vector.tensor_tensor(
                                    flat[:, i, 8 * half:8 * half + 8, kv * NC:(kv + 1) * NC], a,
                                    pos.rearrange("p (j o) -> p j o", o=1).to_broadcast([P, 8, NC]), ALU.add).then_inc(flat_ready, 1)
                    taps(TAPS_PROJ[u])
                    if u < U_KC and u % 2 == 1:
                        t = u // 2
                        done(u)
                        dve.wait_ge(sig_ready, l * CT + (t + 1))
                        nc.vector.tensor_tensor(upad[:, t, PAD:PAD + SEQ], bank[:, 5 + 2 * (t % 2), 0:SEQ],
                                                sig[:, t % 2, :], ALU.mult).then_inc(glu_ready, 1)
                    lo(l, MIX0 + u + RING)
                    if u in PRE_SCORES:
                        if PRE_SCORES[u] == 0:
                            dve.wait_ge(consts_in, 16 * 4)
                        score(PRE_SCORES[u])
                for n in range(N_JOBS):
                    if n + 2 < N_JOBS:
                        score(n + 2)
                    if n < len(TAPS_JOB):
                        taps(TAPS_JOB[n])
                    if n == 5:
                        lo(l, MIX0 + U_W2 + RING)
                    if n == JOB_CMP_SCORES:
                        dve.wait_ge(cscore_done, l + 1)
                        csf = cs[:].rearrange("p a n -> p (a n)")
                        nc.vector.scalar_tensor_tensor(out=csf, in0=bank[:, 7, 0:QT * N_HEADS * NC], scalar=HEAD_DIM ** -0.5,
                                                       in1=calibi[:], op0=ALU.mult, op1=ALU.add).then_inc(cs_step, 1)
                        dve.wait_ge(cs_step, l * 5 + 1)
                        nc.vector.tensor_reduce(cmx[:], cs[:], AX.X, ALU.max).then_inc(cs_step, 1)
                        dve.wait_ge(cs_step, l * 5 + 2)
                        nc.vector.tensor_tensor(cs[:], cs[:], cmx[:].rearrange("p (a o) -> p a o", o=1).to_broadcast([P, QT * N_HEADS, NC]),
                                                ALU.subtract).then_inc(cs_step, 1)
                    if n == JOB_CMP_MASK:
                        dve.wait_ge(ce_ready, l + 1)
                        nc.vector.tensor_reduce(csum[:], ce[:], AX.X, ALU.add).then_inc(cs_step, 1)
                        for qt in range(QT):
                            o = cp[:, qt].rearrange("p kv c n -> p c kv n")[:, :, :, 0:NC]
                            m = cok[:].rearrange("p (t c kv n) -> p t c kv n", t=QT, c=GROUP, kv=N_KV)[:, qt]
                            e = ce[:].rearrange("p (t c kv) n -> p t c kv n", t=QT, c=GROUP)[:, qt]
                            nc.vector.tensor_tensor(o, e, m, ALU.mult).then_inc(cp_ready, 1)
                        dve.wait_ge(cs_step, l * 5 + 4)
                        nc.vector.tensor_copy(cmx[:].rearrange("p (t kv c) -> p t kv c", t=QT, kv=N_KV),
                                              csum[:].rearrange("p (t c kv) -> p t kv c", t=QT, kv=N_KV)).then_inc(cs_step, 1)
                        gsel = gate[:].rearrange("p t (b h) -> p t b h", b=3)
                        dve.wait_ge(cs_step, l * 5 + 5)
                        dve.wait_ge(gate_ready, l + 1)
                        factors(0, cmx[:].rearrange("p (t h) -> p t h", t=QT), gsel[:, :, 0, :], 0)
                    if n == JOB_YSUM:
                        dve.wait_ge(ysum_ready, l + 1)
                        nc.vector.tensor_scalar(mu[:], bank[:, 7, 0:SEQ], 1.0 / CONV_CH, None, ALU.mult).then_inc(mu_ready, 1)
                        dve.wait_ge(mu_ready, l + 1)
                        nc.vector.tensor_tensor(yc[:], y[:], mu[:].rearrange("p (o t) -> p o t", o=1).to_broadcast([P, CT, SEQ]),
                                                ALU.subtract).then_inc(yc_ready, 1)
                    if n == JOB_YVAR:
                        dve.wait_ge(yc_ready, l + 1)
                        nc.vector.tensor_tensor(ysq[:], yc[:], yc[:], ALU.mult).then_inc(ysq_ready, 1)
                    if n == JOB_YNORM:
                        dve.wait_ge(ystd_ready, l + 1)
                        nc.vector.reciprocal(yrstd[:], ystd[:]).then_inc(yrstd_ready, 1)
                        dve.wait_ge(yrstd_ready, l + 1)
                        for t in range(CT):
                            nc.vector.tensor_tensor(yn[:, t, :], yc[:, t, :], yrstd[:], ALU.mult).then_inc(yn_ready, 1)
                    if n == JOB_SELECTED:
                        dve.wait_ge(probs, l * N_JOBS + 6)
                        factors(1, rsum[:, 0], gsel[:, :, 1, :], 2)
                        dve.wait_ge(pv_done, l * N_JOBS + 6)
                        for qt in range(QT):
                            weigh(oacc[:, qt, :], bank[:, qt, :], 1, qt)
                assert next_tap[0] == TAPS
                dve.wait_ge(probs, l * N_JOBS + 12)
                factors(2, rsum[:, 1], gsel[:, :, 2, :], 4)
                dve.wait_ge(pv_done, l * N_JOBS + 12)
                for qt in range(QT):
                    weigh(otmp[:, 0, qt, :], bank[:, 2 + qt, :], 2, qt)
                for t in range(CT):
                    dve.wait_ge(ch_ready, l * CT + (t + 1))
                    nc.vector.tensor_tensor(cl[:, t, :], cz[:, t, :], f32(ch[:, t, :]), ALU.subtract).then_inc(cl_ready, 1)
                dve.wait_ge(cpv_done, l + 1)
                for qt in range(QT):
                    weigh(otmp[:, 1, qt, :], bank[:, 4 + qt, :], 0, qt)
                for b in range(2):
                    for qt in range(QT):
                        dve.wait_ge(o_step, l * 10 + (5 + 2 * b + qt))
                        nc.vector.tensor_tensor(oacc[:, qt], oacc[:, qt], otmp[:, 1 - b, qt], ALU.add).then_inc(o_step, 1)
                for u in range(U_OUT, U_OUT + 2):
                    lo(l, MIX0 + u + RING)
                for b in range(2):
                    dve.wait_ge(ah_ready, l * 2 + b + 1)
                    nc.vector.tensor_tensor(al[:, 2 * b:2 * b + 2, :].rearrange("p a t -> p (a t)"), bank[:, 6 + b, :],
                                            f32(ah[:, 2 * b:2 * b + 2, :]).rearrange("p a t -> p (a t)"),
                                            ALU.subtract).then_inc(al_ready, 1)
                for u in range(U_OUT + 2, MIX_UNITS - 1):
                    lo(l, MIX0 + u + RING)
                residual(l * 12 + 4, 1.0, l * 24 + 16, cur[:, C_N2:C_N2 + KT])
                fold(l * 2 + 1, l * 12 + 8)
                recip(l * 3 + 2)
                ffn(l, 1)

            dve.wait_ge(setup_done, SETUP)
            dve.wait_ge(table_in, 16)
            take_gains(0)
            for b in range(4):
                dve.wait_ge(x_in[b], 16)
                nc.vector.tensor_copy(x[:, 2 * b:2 * b + 2, :], xn[:, 2 * b:2 * b + 2, :]).then_inc(x_ready, 1)
                if b == 0:
                    lo(0, 0)
                    dve.wait_ge(cur_ready, 1)
                if b >= 1:
                    scaled_low(0, cur[:, C_N1:C_N1 + KT], range(2 * b - 2, 2 * b))
            scaled_low(0, cur[:, C_N1:C_N1 + KT], range(KT - 2, KT))
            with dve.Fori(0, DEPTH - 1) as l:
                layer(l, 1)
                take_gains(l + 1)
                for n in range(2):
                    lo(l + 1, n)
                dve.wait_ge(cur_ready, l + 2)
                residual(l * 12 + 8, 0.5, l * 24 + 24, cur[:, C_N1:C_N1 + KT])
            layer(DEPTH - 1, 2)
            residual(DEPTH * 12 - 4, 0.5)
            recip(DEPTH * 3)
            for k in range(KT):
                normed(k, table[:, DEPTH * LAYER_COLS:])

        @block.tensor
        def _(pe):
            mm = nc.tensor.matmul

            def parts(o, n, col, width, a_hi, a_lo, start, stop, more=False):
                s = n % RING
                wh, wl = whi[:, s, col:col + width], wlo[:, s, col:col + width]
                mm(o, wh, a_hi, start=start, stop=False, skip_group_check=more)
                mm(o, wh, a_lo, start=False, stop=False, skip_group_check=more)
                return mm(o, wl, a_hi, start=False, stop=stop, skip_group_check=more)

            def sum_squares(q, q4, to):
                for b in range(4):
                    pe.wait_ge(sq_ready, q4 + (b + 1))
                    for k in (2 * b, 2 * b + 1):
                        m = mm(bank[:, to, 0:SEQ], ones[:], sq[:, k, :], start=(k == 0), stop=(k == KT - 1))
                m.then_inc(ssum_ready, 1)

            def split(at):
                pe.wait_ge(lo_ready, at)

            def project(n, o, width=P, x_from=None):
                for k in range(KT):
                    if x_from is not None:
                        pe.wait_ge(xl_ready, x_from + (k + 1))
                    m = parts(o, n, k * width, width, xh[:, k, :], xl[:, k, :], k == 0, k == KT - 1)
                m.then_inc(unit_used, 1)

            def to_residual(n, a_hi, a_lo, first, last):
                for m8 in range(KT):
                    m = parts(bank[:, m8 // 2, (m8 % 2) * SEQ:(m8 % 2 + 1) * SEQ], n, m8 * P, P, a_hi, a_lo,
                              first and m8 % 2 == 0, last, more=True)
                    if last and m8 % 2 == 1:
                        m.then_inc(y_ready, 1)
                return m

            def ffn(l, f, x8):
                base = FFN2_0 if f else 0

                def gate_up(c, j=None):
                    n, b = base + unit_g(c), 4 + 2 * (c % 2)
                    at, ht = l * LAYER_SPLITS + splits_to(n), l * 2 * FC + (f * FC + c - 1)
                    if j is not None:
                        at, ht = at + j * RING, ht + j * 2
                    if c >= 2:
                        pe.wait_ge(hid_ready, ht)
                    split(at)
                    project(n, bank[:, b, 0:SEQ], x_from=x8 if c == 0 else None)
                    split(at + 1)
                    project(n + 1, bank[:, b + 1, 0:SEQ])
                    if c == 0:
                        pe.wait_ge(folded, l * 4 + f * 2 + 2)
                        for k in range(2):
                            m = mm(bank[:, 0, 0:SEQ], ones[:], sq[:, k, :], start=(k == 0), stop=(k == 1))
                        m.then_inc(ssum_ready, 1)

                def down(c, j=None):
                    n = base + unit_d(c)
                    at, ht = l * LAYER_SPLITS + splits_to(n), l * 2 * FC + (f * FC + c + 1)
                    if j is not None:
                        at, ht = at + j * RING, ht + j * 2
                    pe.wait_ge(hl_ready, ht)
                    split(at)
                    m = to_residual(n, hh[:, c % 2, :], hl[:, c % 2, :], c == 0, c == FC - 1)
                    if c < FC - 1:
                        m.then_inc(unit_used, 1)

                gate_up(0)
                gate_up(1)
                down(0)
                with pe.Fori(0, (FC - 4) // 2) as j:
                    for c in (2, 3):
                        gate_up(c, j)
                        down(c - 1, j)
                gate_up(FC - 2)
                down(FC - 3)
                gate_up(FC - 1)
                down(FC - 2)
                down(FC - 1)
                last_unit()

            def last_unit():
                mm(bank[0:1, 6, 0:1], ones[:, 0:1], ones[:, 0:1], start=True, stop=True).then_inc(unit_used, 1)

            pe.wait_ge(setup_done, SETUP)
            with pe.Fori(0, DEPTH) as l:
                ffn(l, 0, l * 24)
                sum_squares(l * 3 + 1, l * 12 + 4, 7)

                def used(u):
                    split(l * LAYER_SPLITS + splits_to(MIX0 + u))

                for t in range(CT):
                    if t >= 2:
                        pe.wait_ge(glu_ready, l * CT + (t - 1))
                    for i in range(2):
                        used(2 * t + i)
                        project(MIX0 + 2 * t + i, bank[:, 4 + 2 * (t % 2) + i, 0:SEQ],
                                x_from=l * 24 + 8 if t == 0 and i == 0 else None)
                for i in range(4):
                    used(U_KC + i)
                    project(MIX0 + U_KC + i, bank[:, i, 0:SEQ])

                def landed_unit(u):
                    n = MIX0 + u
                    pe.wait_ge(landed[n % RING], l * (16 * LAYER_UNITS // RING) + 16 * (n // RING + 1))

                landed_unit(U_GATE)
                pe.wait_ge(glu_ready, l * CT + 4)
                s = (MIX0 + U_GATE) % RING
                for t in range(QT):
                    for k in range(KT):
                        m = mm(bank[:, 6, t * 24:(t + 1) * 24], xn[:, k, t * P:(t + 1) * P], raw[:, s, k * 24:(k + 1) * 24],
                               start=(k == 0), stop=(k == KT - 1), skip_group_check=True)
                m.then_inc(unit_used, 1)
                for i in range(2):
                    landed_unit(U_V + i)
                    s = (MIX0 + U_V + i) % RING
                    for k4 in range(4):
                        k = 4 * i + k4
                        for t in range(QT):
                            m = mm(bank[:, 4 + t, 0:2 * P], xn[:, k, t * P:(t + 1) * P], raw[:, s, k4 * 2 * P:(k4 + 1) * 2 * P],
                                   start=(k == 0), stop=(k == KT - 1))
                    m.then_inc(unit_used, 1)

                for n in range(8):
                    i, b = divmod(n, 4)
                    if b == 0:
                        pe.wait_ge(flat_ready, l * 8 + 4 * i + 4)
                        if i == 1:
                            pe.wait_ge(gate_ready, l + 1)
                    landed_unit(U_W1K + n)
                    s = (MIX0 + U_W1K + n) % RING
                    for k4 in range(4):
                        k = 4 * b + k4
                        m = mm(bank[0:N_KV * NC, 7 - i, 0:2 * P], flat[:, i, k, :], raw[:, s, k4 * 2 * P:(k4 + 1) * 2 * P],
                               start=(k == 0), stop=(k == 15))
                    m.then_inc(unit_used, 1)

                nb = N_KV * NC

                def turn_hidden():
                    pe.wait_ge(chid_ready, l * 2 + 2)
                    for i in range(4):
                        m = mm(bank[:, 7, i * nb:(i + 1) * nb], chid[:, i // 2, (i % 2) * P:(i % 2 + 1) * P], ident[0:nb, 0:nb],
                               start=True, stop=True, skip_group_check=True)
                    m.then_inc(chid_turned, 1)

                def compress_out():
                    landed_unit(U_W2)
                    w2 = raw[:, (MIX0 + U_W2) % RING, :]
                    pe.wait_ge(chidT_ready, l + 1)
                    for kt in range(2):
                        mm(bank[:, 7, 0:nb], w2[:, kt * P:(kt + 1) * P], chidT[:, kt * nb:(kt + 1) * nb],
                           start=(kt == 0), stop=(kt == 1), skip_group_check=True)
                    for kv in range(N_KV):
                        for kt in range(2):
                            m = mm(bank[0:NC, 7, 64 + 64 * kv:128 + 64 * kv],
                                   chidT[:, (2 + kt) * nb + kv * NC:(2 + kt) * nb + (kv + 1) * NC],
                                   w2[:, 256 + 64 * kt:320 + 64 * kt], start=(kt == 0), stop=(kt == 1), skip_group_check=True)
                    m.then_inc(unit_used, 1)

                def compressed_scores():
                    pe.wait_ge(cmpkv_ready, l * 10 + 10)
                    for t in range(QT):
                        for c in range(GROUP):
                            a = (t * GROUP + c) * nb
                            m = mm(bank[:, 7, a:a + nb], qT[:, c, t * P:(t + 1) * P], kcz[:].rearrange("p a n -> p (a n)"),
                                   start=True, stop=True, skip_group_check=True)
                    m.then_inc(cscore_done, 1)

                def turn_compressed():
                    pe.wait_ge(cp_ready, l * 2 + 2)
                    for i in range(QT * N_KV):
                        m = nc.tensor.transpose(bank[:, 7, i * P:(i + 1) * P],
                                                cp[:, i // N_KV, i % N_KV].rearrange("p c n -> p (c n)"), ident[:])
                    m.then_inc(cp_turned, 1)

                def sum_channels(src):
                    for t in range(CT):
                        m = mm(bank[:, 7, 0:SEQ], ones[:], src[:, t, :], start=(t == 0), stop=(t == CT - 1))
                    return m

                def scores(n):
                    br, qt, segs = job(n)
                    if n >= 2:
                        pe.wait_ge(scored, l * N_JOBS + (n - 1))
                    if qt == 1:
                        m = mm(bank[:, 4 + n % 2, :], qT[:, segs[0][0], P:2 * P], kz[:, br].rearrange("p a t -> p (a t)"),
                               start=True, stop=True)
                    else:
                        for i in range(2):
                            m = mm(bank[:, 4 + n % 2, 2 * P * i:2 * P * (i + 1)], qT[:, segs[2 * i][0], 0:P], kz[:, br, :, 0:P],
                                   start=True, stop=True, skip_group_check=True)
                    m.then_inc(scores_done, 1)

                def turn(n):
                    pe.wait_ge(probs, l * N_JOBS + (n + 1))
                    if n >= 1:
                        pe.wait_ge(prT_ready, l * N_JOBS + n)
                    for i in range(4):
                        m = nc.tensor.transpose(bank[:, 6, i * P:(i + 1) * P], pr[n % PR][:, i * P:(i + 1) * P], ident[:])
                    m.then_inc(turned, 1)

                def values(n):
                    br, qt, segs = job(n)
                    pe.wait_ge(prT_ready, l * N_JOBS + (n + 1))
                    at = 0
                    for h, kb in segs:
                        kv = h // GROUP
                        for b in range(kb):
                            m = mm(bank[:, 2 * br + qt, h * HEAD_DIM:(h + 1) * HEAD_DIM], prT[:, n % 2, at:at + P],
                                   v[:, b, br * P + kv * 64:br * P + kv * 64 + 64],
                                   start=(b == 0 and segs[0][0] == 0 and h == 0), stop=(b == kb - 1), skip_group_check=True)
                            at += P
                    m.then_inc(pv_done, 1)

                pe.wait_ge(kk_ready, l * 8 + 8)
                pe.wait_ge(kz_ready, l * 4 + 4)
                pe.wait_ge(v_ready, l * 2 + 2)
                pe.wait_ge(consts_in, 16 * 4)
                for c in range(GROUP):
                    used(U_Q + c)
                    project(MIX0 + U_Q + c, bank[:, c, 0:SEQ])
                    if c == 1:
                        turn_hidden()
                    if U_Q + c in PRE_SCORES:
                        pe.wait_ge(q_ready, l * 4 + (PRE_SCORES[U_Q + c] + 1))
                        scores(PRE_SCORES[U_Q + c])
                compress_out()
                pe.wait_ge(q_ready, l * 4 + 4)
                for n in range(N_JOBS):
                    if n + 2 < N_JOBS:
                        scores(n + 2)
                    turn(n)
                    if n == JOB_CMP_SCORES:
                        compressed_scores()
                    if n == JOB_CMP_TURN:
                        turn_compressed()
                    if n == JOB_YSUM:
                        pe.wait_ge(tap_done, l * TAPS + TAPS)
                        pe.wait_ge(cpT_ready, l + 1)
                        sum_channels(y).then_inc(ysum_ready, 1)
                    if n == JOB_YVAR + 1:
                        pe.wait_ge(ysq_ready, l + 1)
                        sum_channels(ysq).then_inc(yvar_ready, 1)
                    if n >= 1:
                        values(n - 1)
                values(N_JOBS - 1)
                for i in range(QT * N_KV):
                    t, kv = divmod(i, N_KV)
                    m = mm(bank[:, 4 + t, kv * 256:(kv + 1) * 256], cpT[:, t, kv, :], vcd[:, kv, :], start=True, stop=True,
                           skip_group_check=True)
                m.then_inc(cpv_done, 1)
                pe.wait_ge(o_step, l * 10 + 4)
                pe.wait_ge(ystd_ready, l + 1)
                for t in range(CT):
                    used(U_OUT + t)
                    pe.wait_ge(cl_ready, l * CT + t + 1)
                    to_residual(MIX0 + U_OUT + t, ch[:, t, :], cl[:, t, :], t == 0, False).then_inc(unit_used, 1)
                    if t == 2:
                        pe.wait_ge(o_step, l * 10 + 10)
                        for i in range(4):
                            for qt in range(QT):
                                m = nc.tensor.transpose(bank[:, 6 + i // 2, (i % 2) * SEQ + qt * P:(i % 2) * SEQ + (qt + 1) * P],
                                                        oacc[:, qt, i * P:(i + 1) * P], ident[:])
                        m.then_inc(o_turned, 1)
                for t in range(4):
                    used(U_OUT + 4 + t)
                    pe.wait_ge(al_ready, l * 2 + t // 2 + 1)
                    m = to_residual(MIX0 + U_OUT + 4 + t, ah[:, t, :], al[:, t, :], False, t == 3)
                    if t < 3:
                        m.then_inc(unit_used, 1)
                last_unit()
                ffn(l, 1, l * 24 + 16)
            sum_squares(DEPTH * 3, DEPTH * 12, 7)


def _columns(wt, cols):
    import numpy as np
    a = wt[:, cols].reshape(-1, 128, len(cols)).transpose(1, 0, 2).reshape(128, -1)
    u = np.zeros((128, 1024), np.float32)
    u[:, :a.shape[1]] = a
    return u


def _stream(a):
    import numpy as np
    units = []
    for l in range(2):
        def ffn(g, u, d):
            g, u, d = a[g][l], a[u][l], a[d][l]
            def gu(c):
                cols = np.arange(c * 128, (c + 1) * 128)
                units.append(_columns(g, cols))
                units.append(_columns(u, cols))
            gu(0)
            for c in range(1, 22):
                gu(c)
                units.append(d[(c - 1) * 128:c * 128])
            units.append(d[21 * 128:])
        ffn("ffn1_w_gate", "ffn1_w_up", "ffn1_w_down")
        w = a["w_in"][l]
        q0, kc, vc, ks, vs, kw, vw, gl, ga, gb = np.cumsum([0, 512, 128, 128, 128, 128, 128, 128, 24, 512])
        r = np.arange
        for t in range(4):
            units.append(_columns(w, gb + t * 128 + r(128)))
            units.append(_columns(w, ga + t * 128 + r(128)))
        for o in (kc, vc, ks, kw):
            units.append(_columns(w, o + r(128)))
        units.append(_columns(w, gl + np.array([h * 3 + b for b in range(3) for h in range(8)])))
        vv = np.concatenate([vs + r(128), vw + r(128)])
        units.append(_columns(w[:512], vv))
        units.append(_columns(w[512:], vv))
        for n in ("cmp_k_w1", "cmp_v_w1"):
            for b in range(4):
                units.append(_columns(a[n][l][b * 512:(b + 1) * 512], r(256)))
        for c in range(4):
            units.append(_columns(w, np.concatenate([q0 + c * 64 + r(64), q0 + (c + 4) * 64 + r(64)])))
        u = np.zeros((128, 1024), np.float32)
        for kt in range(2):
            k2 = a["cmp_k_w2"][l][kt * 128:(kt + 1) * 128]
            u[:, kt * 128:kt * 128 + 64] = k2
            u[:, kt * 128 + 64:kt * 128 + 128] = k2
            u[:, 256 + kt * 64:320 + kt * 64] = a["cmp_v_w2"][l][kt * 128:(kt + 1) * 128]
        units.append(u)
        for t in (4, 5, 6, 7, 0, 1, 2, 3):
            units.append(a["w_out"][l][t * 128:(t + 1) * 128])
        ffn("ffn2_w_gate", "ffn2_w_up", "ffn2_w_down")
    return np.stack(units)


def _params(a):
    import numpy as np
    cols = []
    tile = lambda vec: vec.reshape(-1, 128)
    for l in range(2):
        for n in ("ffn1_norm", "mix_norm", "ffn2_norm", "conv_b", "conv_norm_g", "conv_norm_b"):
            cols.append(tile(a[n][l]))
        cols.append(tile(a["conv_w"][l]))
        cols.append(tile(a["cmp_pos_k"][l]))
        cols.append(tile(a["cmp_pos_v"][l]))
    cols.append(tile(a["final_norm"]))
    return np.ascontiguousarray(np.concatenate(cols).T)


def _tables():
    import numpy as np
    slope = 2.0 ** (-8.0 * np.arange(1, 9) / 8)
    q, k = np.arange(128)[:, None], np.arange(256)[None]
    d = 128 + q - k
    bias = np.where(d[:, None, :] >= 0, -8.0 * slope[None, :, None] * d[:, None, :], -1e31).astype(np.float32)
    t = (np.arange(2)[None, :, None] * 128 + np.arange(128)[:, None, None])
    end = (np.arange(15) * 16 + 31)[None, None, :]
    dc = t - end
    sl = slope.reshape(2, 4).T.reshape(8)
    full = np.broadcast_to(dc[:, :, None, :], (128, 2, 8, 15))
    cb = np.where(full >= 0, -sl[None, None, :, None] * full, -1e30).astype(np.float32).reshape(128, 240)
    ok = (full >= 0).astype(np.float32).reshape(128, 240)
    return np.ascontiguousarray(bias), np.ascontiguousarray(cb), np.ascontiguousarray(ok)


def kernel(**inputs):
    import numpy as np
    import concourse.bacc as bacc
    from concourse.bass_utils import run_bass_kernel_spmd

    a = {k: np.asarray(v) for k, v in inputs.items()}
    bias, cb, ok = _tables()
    xT = np.ascontiguousarray(a["x"][0].T.reshape(8, 128, 256).transpose(1, 0, 2))
    arrays = {"w": _stream(a), "xT": xT, "params": _params(a), "bias": bias, "cbias": cb, "cmask": ok,
              "eye": np.eye(128, dtype=np.float32)}
    nc = bacc.Bacc("TRN2", target_bir_lowering=False, num_devices=1)
    aps = [nc.dram_tensor(n, v.shape, F32, kind="ExternalInput").ap() for n, v in arrays.items()]
    out = nc.dram_tensor("outT", (128, 8, 256), F32, kind="ExternalOutput").ap()
    trunk(nc, *aps, out)
    r = run_bass_kernel_spmd(nc, [arrays], core_ids=[0])
    o = r.results[0]["outT"]
    return np.ascontiguousarray(o.transpose(1, 0, 2).reshape(1024, 256).T)[None]
```
